# Optimizing a Trainium2 kernel written in Bass

```python
import math
import jax, jax.numpy as jnp
from jax import lax
import numpy as np

D_MODEL = 1024
BATCH = 1
SEQ = 256
DEPTH = 2

D_MIX = D_MODEL
DIFF_HEADS = 4
DIFF_QK_DIM = D_MIX // 16
DIFF_V_DIM = 2 * DIFF_QK_DIM
RET_HEADS = 4
RET_K_DIM = D_MIX // 16
RET_V_DIM = D_MIX // 8
D_FF = ((8 * D_MODEL // 3 + 255) // 256) * 256
Q_BLOCK = 128
RET_CHUNK = 128
NORM_EPS = 1e-6
HALF_STEP = 0.5
LAMBDA_INIT_STD = 0.1

DIFF_QK_W = DIFF_HEADS * 2 * DIFF_QK_DIM
DIFF_V_W = DIFF_HEADS * DIFF_V_DIM
RET_QK_W = RET_HEADS * RET_K_DIM
RET_V_W = RET_HEADS * RET_V_DIM
IN_COLS = 2 * DIFF_QK_W + DIFF_V_W + 2 * RET_QK_W + 2 * RET_V_W
OUT_ROWS = DIFF_V_W + RET_V_W

kernel_name = 'hymba_diffattn_retention_macaron'

def rmsnorm(x, g):
    xf = x.astype(jnp.float32)
    y = xf * lax.rsqrt(jnp.mean(xf * xf, axis=-1, keepdims=True) + NORM_EPS)
    return (y * g.astype(jnp.float32)).astype(x.dtype)

def head_rms(x):
    return x * lax.rsqrt(jnp.mean(x * x, axis=-1, keepdims=True) + NORM_EPS)

def swiglu(x, w_gate, w_up, w_down):
    return (jax.nn.silu(x @ w_gate) * (x @ w_up)) @ w_down

def alibi_slopes(n_heads):
    return jnp.asarray(2.0 ** (-8.0 * np.arange(1, n_heads + 1) / n_heads), dtype=jnp.float32)

def retention_log_decay(n_heads):
    return jnp.asarray(np.log(1.0 - 2.0 ** (-5.0 - np.arange(n_heads))), dtype=jnp.float32)

def diff_heads(t, B, S):
    return jnp.transpose(t.reshape(B, S, DIFF_HEADS, 2, DIFF_QK_DIM), (0, 2, 3, 1, 4))

def diff_attention(q, k, v, lam, lam_init, subln_g):
    B, H, _, S, d = q.shape
    dv = v.shape[-1]
    nb = S // Q_BLOCK
    scale = d ** -0.5
    slopes = alibi_slopes(H)
    key_pos = jnp.arange(S)
    q_blocks = jnp.moveaxis(q.reshape(B, H, 2, nb, Q_BLOCK, d), 3, 0)
    g = subln_g.astype(jnp.float32)

    def block(args):
        idx, qb = args
        q_pos = idx * Q_BLOCK + jnp.arange(Q_BLOCK)
        dist = (q_pos[:, None] - key_pos[None, :]).astype(jnp.float32)
        bias = -slopes[:, None, None] * dist
        s = jnp.einsum('bhcqd,bhckd->bhcqk', qb, k).astype(jnp.float32) * scale + bias[None, :, None]
        s = jnp.where(dist >= 0, s, -jnp.inf)
        p = jax.nn.softmax(s, axis=-1)
        probs = p[:, :, 0] - lam * p[:, :, 1]
        o = jnp.einsum('bhqk,bhkv->bhqv', probs.astype(v.dtype), v).astype(jnp.float32)
        return head_rms(o) * g * (1.0 - lam_init)

    out = lax.map(block, (jnp.arange(nb), q_blocks))
    return jnp.transpose(out, (1, 0, 3, 2, 4)).reshape(B, S, H * dv)

def retention(q, k, v):
    B, S, H, dk = q.shape
    dv = v.shape[-1]
    C = RET_CHUNK
    N = S // C
    lg = retention_log_decay(H)
    q = q.reshape(B, N, C, H, dk)
    k = k.reshape(B, N, C, H, dk) * (dk ** -0.5)
    v = v.reshape(B, N, C, H, dv)
    pos = jnp.arange(C, dtype=jnp.float32)
    rel = pos[:, None] - pos[None, :]
    intra = jnp.where(rel >= 0, jnp.exp(lg[:, None, None] * rel), 0.0)
    scores = jnp.einsum('bnihd,bnjhd->bnhij', q, k) * intra
    inner = jnp.einsum('bnhij,bnjhv->bnihv', scores, v)
    tail = jnp.exp(lg[:, None] * (C - 1.0 - pos))
    kv = jnp.einsum('bnjhd,bnjhv,hj->nbhdv', k, v, tail)
    chunk_decay = jnp.exp(lg * C)[None, :, None, None]

    def step(state, kv_n):
        return state * chunk_decay + kv_n, state

    _, prev = lax.scan(step, jnp.zeros(kv.shape[1:], kv.dtype), kv)
    head = jnp.exp(lg[:, None] * (pos + 1.0))
    cross = jnp.einsum('bnihd,nbhdv,hi->bnihv', q, prev, head)
    o = (inner + cross).astype(jnp.float32)
    return head_rms(o).reshape(B, S, H * dv)

def setup_inputs(seed: int = 0) -> dict:
    key = jax.random.key(seed)
    ks = jax.random.split(key, 20)
    f32 = jnp.float32

    def normal(k, shape, scale):
        return jax.random.normal(k, shape, f32) * scale

    def gain(k, shape):
        return 1.0 + 0.02 * jax.random.normal(k, shape, f32)

    return {
        'x': normal(ks[0], (BATCH, SEQ, D_MODEL), 1.0),
        'norm_ffn1': gain(ks[1], (DEPTH, D_MODEL)),
        'w1_gate': normal(ks[2], (DEPTH, D_MODEL, D_FF), D_MODEL ** -0.5),
        'w1_up': normal(ks[3], (DEPTH, D_MODEL, D_FF), D_MODEL ** -0.5),
        'w1_down': normal(ks[4], (DEPTH, D_FF, D_MODEL), D_FF ** -0.5),
        'norm_mix': gain(ks[5], (DEPTH, D_MODEL)),
        'w_in': normal(ks[6], (DEPTH, D_MODEL, IN_COLS), D_MODEL ** -0.5),
        'lambda_q1': normal(ks[7], (DEPTH, DIFF_QK_DIM), LAMBDA_INIT_STD),
        'lambda_k1': normal(ks[8], (DEPTH, DIFF_QK_DIM), LAMBDA_INIT_STD),
        'lambda_q2': normal(ks[9], (DEPTH, DIFF_QK_DIM), LAMBDA_INIT_STD),
        'lambda_k2': normal(ks[10], (DEPTH, DIFF_QK_DIM), LAMBDA_INIT_STD),
        'diff_subln': gain(ks[11], (DEPTH, DIFF_V_DIM)),
        'w_out': normal(ks[12], (DEPTH, OUT_ROWS, D_MODEL), OUT_ROWS ** -0.5),
        'norm_ffn2': gain(ks[13], (DEPTH, D_MODEL)),
        'w2_gate': normal(ks[14], (DEPTH, D_MODEL, D_FF), D_MODEL ** -0.5),
        'w2_up': normal(ks[15], (DEPTH, D_MODEL, D_FF), D_MODEL ** -0.5),
        'w2_down': normal(ks[16], (DEPTH, D_FF, D_MODEL), D_FF ** -0.5),
        'norm_final': gain(ks[17], (D_MODEL,)),
    }

def reference(x, norm_ffn1, w1_gate, w1_up, w1_down, norm_mix, w_in, lambda_q1, lambda_k1, lambda_q2, lambda_k2, diff_subln, w_out, norm_ffn2, w2_gate, w2_up, w2_down, norm_final):
    B, S, _ = x.shape
    split_at = np.cumsum([DIFF_QK_W, DIFF_QK_W, DIFF_V_W, RET_QK_W, RET_QK_W, RET_V_W]).tolist()
    for l in range(DEPTH):
        x = x + HALF_STEP * swiglu(rmsnorm(x, norm_ffn1[l]), w1_gate[l], w1_up[l], w1_down[l])
        h = rmsnorm(x, norm_mix[l])
        proj = h @ w_in[l]
        dq, dk, dv, rq, rk, rv, rg = jnp.split(proj, split_at, axis=-1)
        lam_init = 0.8 - 0.6 * math.exp(-0.3 * l)
        lam = (jnp.exp(jnp.sum(lambda_q1[l].astype(jnp.float32) * lambda_k1[l].astype(jnp.float32)))
               - jnp.exp(jnp.sum(lambda_q2[l].astype(jnp.float32) * lambda_k2[l].astype(jnp.float32)))
               + lam_init)
        v_heads = jnp.transpose(dv.reshape(B, S, DIFF_HEADS, DIFF_V_DIM), (0, 2, 1, 3))
        o_diff = diff_attention(diff_heads(dq, B, S), diff_heads(dk, B, S), v_heads, lam, lam_init, diff_subln[l])
        o_ret = retention(rq.reshape(B, S, RET_HEADS, RET_K_DIM),
                          rk.reshape(B, S, RET_HEADS, RET_K_DIM),
                          rv.reshape(B, S, RET_HEADS, RET_V_DIM))
        o_ret = jax.nn.silu(rg.astype(jnp.float32)) * o_ret
        mixed = jnp.concatenate([o_diff, o_ret], axis=-1).astype(x.dtype)
        x = x + mixed @ w_out[l]
        x = x + HALF_STEP * swiglu(rmsnorm(x, norm_ffn2[l]), w2_gate[l], w2_up[l], w2_down[l])
    return rmsnorm(x, norm_final)


_drawn_inputs = setup_inputs


def setup_inputs(seed=0):
    import zlib

    import numpy as np

    out = dict(_drawn_inputs(seed))
    spreads = {}
    factors = {'norm_ffn1': 3.58,
     'lambda_q2': 4.459,
     'diff_subln': 13.26,
     'norm_ffn2': 5.569,
     'norm_final': 8.251}
    for name, (base, spread) in spreads.items():
        noise = np.random.default_rng([zlib.crc32(name.encode()), seed]).standard_normal(out[name].shape)
        drawn = base * np.exp(spread * noise) if base else spread * noise
        out[name] = __import__('jax').numpy.asarray(drawn.astype(out[name].dtype))
    for name, factor in factors.items():
        out[name] = (out[name] * factor).astype(out[name].dtype)
    return out
```

```python
from contextlib import ExitStack

import numpy as np
import concourse.bass as bass
from concourse import mybir

F32 = mybir.dt.float32
F32R = mybir.dt.float32r
BF16 = mybir.dt.bfloat16
ALU = mybir.AluOpType
ACT = mybir.ActivationFunctionType

P = 128
D, SEQ, DEPTH = 1024, 256, 2
TT = SEQ // P
KT = D // P
F = ((8 * D // 3 + 255) // 256) * 256
CH = 256
STEPS = F // CH
HEADS = 4
QK = D // 16
V = 2 * QK
EPS = 1e-6
MASKED = -3.0e38
SCALE = QK ** -0.5

PIECE = 2048
RAW, SLOTS = 3, 6
AHEAD = 2
FFN_PIECES = 3 * STEPS
PROJ = 6
MIX_PIECES = 2 * (PROJ - 1) + 4 + 4
MIX0 = FFN_PIECES
FFN2 = MIX0 + MIX_PIECES
LP = FFN2 + FFN_PIECES
assert LP % SLOTS == 0 and STEPS % 2 == 1
LOOPED = (STEPS - 3) // 2
W0 = 2 * (PROJ - 1) + 4

SLOPES = [2.0 ** (-8.0 * (h + 1) / HEADS) for h in range(HEADS)]
LOG_DECAY = [float(np.log(1.0 - 2.0 ** (-5.0 - h))) for h in range(HEADS)]
LAM_INIT = [0.8 - 0.6 * float(np.exp(-0.3 * l)) for l in range(DEPTH)]


def build(nc, x_in, norm_ffn1, w1_gate, w1_up, w1_down, norm_mix, w_in, lam_q1, lam_k1, lam_q2, lam_k2,
          subln, w_out, norm_ffn2, w2_gate, w2_up, w2_down, norm_final, out):
    ctx = ExitStack()
    with ctx:
        def sb(name, shape, dt=F32):
            return ctx.enter_context(nc.sbuf_tensor(name, shape, dt))

        def sem(name):
            return ctx.enter_context(nc.semaphore(name))

        raw = sb("raw", [P, RAW, PIECE])
        w_hi = sb("w_hi", [P, SLOTS, PIECE], F32R)
        w_lo = sb("w_lo", [P, SLOTS, PIECE], F32R)
        x = sb("x", [P, TT, D])
        wide = sb("wide", [P, TT, D])
        xT_hi = sb("xT_hi", [P, KT, SEQ], F32R)
        xT_lo = sb("xT_lo", [P, KT, SEQ], F32R)
        aT_hi = sb("aT_hi", [P, 4, SEQ], F32R)
        aT_lo = sb("aT_lo", [P, 4, SEQ], F32R)
        gain = sb("gain", [P, D])
        hid = sb("hid", [P, 1024])
        silu_g = hid[:, 0:512].rearrange("p (t n) -> p t n", t=TT)
        hidden = hid[:, 512:1024].rearrange("p (t n) -> p t n", t=TT)
        dv = sb("dv", [P, TT, 512])
        rqk = sb("rqk", [P, TT, 512])
        rv = sb("rv", [P, TT, 512])
        gate = sb("gate", [P, TT, 512])
        qT = sb("qT", [P, HEADS, SEQ])
        kT = sb("kT", [P, HEADS, SEQ])
        rT = sb("rT", [P, 4, SEQ])
        bias8 = sb("bias8", [P, HEADS, SEQ])
        decay = sb("decay", [P, HEADS, SEQ])
        ident = sb("ident", [P, P])
        lams = qT[:, 0:2, :].rearrange("p a (b n) -> p (a b) n", b=2)
        gsub2 = sb("gsub2", [P, DEPTH, V])
        gsub = sb("gsub", [P, V])
        st = sb("st", [P, 64])
        ssq, rstd, tmp = st[:, 0:2], st[:, 2:4], st[:, 4:8]
        neg_half = st[:, 8:12]
        lam_dot, lam_exp, neg_lams, neg_lam = st[:, 12:16], st[:, 16:20], st[:, 20:22], st[:, 22:23]
        mx, nmx, sums, rec = (st[:, a:a + 8] for a in (24, 32, 40, 48))
        hn = sb("hn", [P, 48])
        h_ssq, h_tmp, h_rstd = hn[:, 0:16], hn[:, 16:32], hn[:, 32:48]
        junk = rT[:, :, :].rearrange("p a n -> p (a n)")
        zeros = junk[:, 0:256].bitcast(BF16)
        dq_dk = wide

        def z(h, c, a, b):
            o = ((h % 2) * 2 + c) * 384
            return wide[:, :, :].rearrange("p t n -> p (t n)")[:, o + a:o + b]

        def probsT(h, a, b):
            t = (qT, kT)[h % 2]
            return t[:, 2 * (h // 2):2 * (h // 2) + 2, :].rearrange("p a n -> p (a n)")[:, a:b]

        def retT(h, a, b):
            t = hid[:, :] if h < 2 else rqk[:, :, :].rearrange("p t n -> p (t n)")
            return t[:, (h % 2) * 384 + a:(h % 2) * 384 + b]

        acc = [ctx.enter_context(nc.psum_tensor(f"acc{i}", [P, 512], F32)) for i in range(4)]
        gu = [ctx.enter_context(nc.psum_tensor(f"gu{i}", [P, 512], F32)) for i in range(2)]
        tp = [ctx.enter_context(nc.psum_tensor(f"tp{i}", [P, 512], F32)) for i in range(2)]

        raw_loaded = [sem(f"raw_loaded{i}") for i in range(RAW)]
        x_loaded, lam_loaded, gain_loaded, out_stored = (sem(n) for n in ("x_loaded", "lam_loaded", "gain_loaded", "out_stored"))
        consts_made, pool_steps, decay_exp, lam_steps, lam_exped = (sem(n) for n in ("consts_made", "pool_steps", "decay_exp", "lam_steps", "lam_exped"))
        hi_done = sem("hi_done")
        lo_done = sem("lo_done")
        slot_free = sem("slot_free")
        acc_ready, x_new, xg_ready, sq_done, rstd_done, xT_psum, xT_hi_done, xT_lo_done = (
            sem(n) for n in ("acc_ready", "x_new", "xg_ready", "sq_done", "rstd_done", "xT_psum", "xT_hi_done", "xT_lo_done"))
        rstd_tmp = sem("rstd_tmp")
        gu_ready, silu_done, hidden_done, hT_psum, hT_hi_done, hT_lo_done = (
            sem(n) for n in ("gu_ready", "silu_done", "hidden_done", "hT_psum", "hT_hi_done", "hT_lo_done"))
        proj_ready, proj_read = sem("proj_ready"), sem("proj_read")
        qkT_psum, qkT_done = sem("qkT_psum"), sem("qkT_done")
        scores_ready, max_done, negmax_done, exp_done, rec_steps, probs_part, probs_done = (
            sem(n) for n in ("scores_ready", "max_done", "negmax_done", "exp_done", "rec_steps", "probs_part", "probs_done"))
        probsT_psum, probsT_done, pv_ready, o_sq_done, o_rstd_done, o_done = (
            sem(n) for n in ("probsT_psum", "probsT_done", "pv_ready", "o_sq_done", "o_rstd_done", "o_done"))
        ret_ready, retT_done, ro_ready, ro_sq_done, ro_rstd_done, ro_done = (
            sem(n) for n in ("ret_ready", "retT_done", "ro_ready", "ro_sq_done", "ro_rstd_done", "ro_done"))
        head_tmp = sem("head_tmp")
        mT_psum, mT_hi_done, mT_lo_done = sem("mT_psum"), sem("mT_hi_done"), sem("mT_lo_done")
        layer_vals, scores_seen = sem("layer_vals"), sem("scores_seen")

        block = ctx.enter_context(nc.Block())
        PHASES = 3

        @block.sync
        def _(sp):
            sp.sem_inc(lo_done, RAW)
            sp.dma_start(x[:, :, :], x_in[0, :, :].rearrange("(t p) n -> p t n", p=P)).then_inc(x_loaded, 16)

            def load(layer, it, pos, srcs, n=PIECE):
                sp.wait_ge(lo_done, LP * layer + SLOTS * it + pos + 1)
                dst = raw[:, pos % RAW, 0:n]
                for half, src in enumerate(srcs):
                    if len(srcs[0].shape) == 3 and srcs[0].shape[1] == 4:
                        d = dst.rearrange("p (k g n) -> p k g n", k=4, g=2)[:, :, half, :]
                    else:
                        d = dst[:, half * n // 2:(half + 1) * n // 2]
                        if len(src.shape) == 3:
                            d = d.rearrange("p (k n) -> p k n", k=src.shape[1])
                    sp.dma_start(d, src).then_inc(raw_loaded[pos % RAW], 16)

            def ffn(layer, base, wg, wu, wd):
                def load_gu(it, pos, j):
                    for h in range(2):
                        rows = [w[layer, h * 512:(h + 1) * 512, bass.ds(j * CH, CH)].rearrange("(k p) n -> p k n", p=P)
                                for w in (wg, wu)]
                        load(layer, it, base + pos + h, rows)

                def load_down(it, pos, j):
                    load(layer, it, base + pos, [wd[layer, bass.ds(j * CH + k * P, P), :] for k in range(2)])

                load_gu(0, 0, 0)
                load_gu(0, 2, 1)
                load_down(0, 4, 0)
                with sp.Fori(0, LOOPED) as it:
                    for u in range(2):
                        load_gu(it, 5 + 3 * u, 2 * it + 2 + u)
                        load_down(it, 7 + 3 * u, 2 * it + 1 + u)
                e = FFN_PIECES - 4
                load_gu(0, e, STEPS - 1)
                load_down(0, e + 2, STEPS - 2)
                load_down(0, e + 3, STEPS - 1)

            with sp.Fori(0, DEPTH) as layer:
                ffn(layer, 0, w1_gate, w1_up, w1_down)
                for c in range(PROJ):
                    parts = 2 if c < PROJ - 1 else 4
                    kk = KT // parts
                    for h in range(parts):
                        srcs = [w_in[layer, (h * kk + g * kk // 2) * P:(h * kk + (g + 1) * kk // 2) * P,
                                     c * 512:(c + 1) * 512] for g in range(2)]
                        if kk == 4:
                            srcs = [s.rearrange("(k p) n -> p k n", p=P) for s in srcs]
                        load(layer, 0, MIX0 + 2 * c + h, srcs, kk * 512)
                for w in range(4):
                    load(layer, 0, MIX0 + W0 + w, [w_out[layer, (2 * w + k) * P:(2 * w + k + 1) * P, :] for k in range(2)])
                ffn(layer, FFN2, w2_gate, w2_up, w2_down)
            for tt in range(TT):
                sp.wait_ge(xg_ready, 4 * PHASES * DEPTH + 2 * TT + tt + 1)
                sp.dma_start(out[0, tt * P:(tt + 1) * P, :], x[:, tt, :]).then_inc(out_stored, 16)
            sp.wait_ge(out_stored, 16 * TT)

        @block.gpsimd
        def _(pool):
            def load_gain(src):
                pool.dma_start(gain[:, :], src.partition_broadcast(P)).then_inc(gain_loaded, 16)

            def entry(q, tt):
                pool.wait_ge(sq_done, TT * q + tt + 1)
                nc.gpsimd.tensor_scalar(tmp[:, tt:tt + 1], ssq[:, tt:tt + 1], 1.0 / D, EPS, ALU.mult, ALU.add).then_inc(rstd_tmp, 1)
                pool.wait_ge(rstd_tmp, TT * q + tt + 1)
                nc.gpsimd.tensor_tensor(rstd[:, tt:tt + 1], tmp[:, tt:tt + 1], neg_half[:, 0:1], ALU.pow).then_inc(rstd_done, 1)

            def head_factor(layer, i, when, count, done):
                fs = slice(4 * i, 4 * i + 4)
                pool.wait_ge(when, count)
                nc.gpsimd.tensor_scalar(h_tmp[:, fs], h_ssq[:, fs], 1.0 / V, EPS, ALU.mult, ALU.add).then_inc(head_tmp, 1)
                pool.wait_ge(head_tmp, 4 * layer + i + 1)
                nc.gpsimd.tensor_tensor(h_rstd[:, fs], h_tmp[:, fs], neg_half, ALU.pow).then_inc(done, 1)

            load_gain(norm_ffn1[0, :])
            for i, lam in enumerate((lam_q1, lam_k1, lam_q2, lam_k2)):
                pool.dma_start(lams[:, i, :], lam.rearrange("l n -> (l n)").partition_broadcast(P)).then_inc(lam_loaded, 16)
            pool.dma_start(gsub2[:, :, :].rearrange("p l n -> p (l n)"),
                           subln.rearrange("l n -> (l n)").partition_broadcast(P)).then_inc(lam_loaded, 16)
            nc.gpsimd.memset(ident[:, :], 0.0).then_inc(pool_steps, 1)
            nc.gpsimd.memset(neg_half, -0.5).then_inc(pool_steps, 1)
            nc.gpsimd.iota(decay[:, :, :], pattern=[[0, HEADS], [1, SEQ]], base=0, channel_multiplier=-1,
                           allow_small_or_imprecise_dtypes=True).then_inc(pool_steps, 1)
            pool.wait_ge(pool_steps, 3)
            nc.gpsimd.affine_select(out=ident[:, :], in_=ident[:, :], compare_op=ALU.not_equal, fill=1.0, base=0,
                                    pattern=[[-1, P]], channel_multiplier=1).then_inc(consts_made, 1)
            for tt in range(TT):
                entry(0, tt)
            nc.gpsimd.iota(bias8[:, :, :], pattern=[[0, HEADS], [-1, SEQ]], base=P, channel_multiplier=1,
                           allow_small_or_imprecise_dtypes=True).then_inc(pool_steps, 1)
            pool.wait_ge(pool_steps, 4)
            for h in range(HEADS):
                nc.gpsimd.tensor_scalar(bias8[:, h, :], bias8[:, h, :], -SLOPES[h] / SCALE, None, ALU.mult).then_inc(pool_steps, 1)
            pool.wait_ge(decay_exp, HEADS)
            nc.gpsimd.tensor_scalar(decay[:, :, :], decay[:, :, :], SCALE, None, ALU.mult).then_inc(pool_steps, 1)
            pool.wait_ge(pool_steps, 5 + HEADS)
            nc.gpsimd.affine_select(out=bias8[:, :, :], in_=bias8[:, :, :], compare_op=ALU.is_ge, fill=MASKED, base=P,
                                    pattern=[[0, HEADS], [-1, SEQ]], channel_multiplier=1).then_inc(consts_made, 1)
            nc.gpsimd.affine_select(out=decay[:, :, :], in_=decay[:, :, :], compare_op=ALU.is_ge, fill=0.0, base=0,
                                    pattern=[[0, HEADS], [1, SEQ]], channel_multiplier=-1).then_inc(consts_made, 1)

            def next_gain(q, src):
                pool.wait_ge(xg_ready, 4 * q + 4)
                load_gain(src)

            def mixer_and_ffn2_entry(layer):
                for tt in range(TT):
                    entry(3 * layer + 1, tt)
                next_gain(3 * layer + 1, norm_ffn2[layer, :])
                for pair in range(2):
                    head_factor(layer, pair, o_sq_done, 2 * layer + pair + 1, o_rstd_done)
                for tt in range(TT):
                    head_factor(layer, 2 + tt, ro_sq_done, 2 * layer + tt + 1, ro_rstd_done)
                for tt in range(TT):
                    entry(3 * layer + 2, tt)

            next_gain(0, norm_mix[0, :])
            mixer_and_ffn2_entry(0)
            if DEPTH > 1:
                with pool.Fori(1, DEPTH) as layer:
                    next_gain(3 * layer - 1, norm_ffn1[layer, :])
                    for tt in range(TT):
                        entry(3 * layer, tt)
                    next_gain(3 * layer, norm_mix[layer, :])
                    mixer_and_ffn2_entry(layer)
            next_gain(3 * DEPTH - 1, norm_final[:])
            for tt in range(TT):
                entry(3 * DEPTH, tt)

        @block.scalar
        def _(act):
            def split_hi(layer, pos, it=0, n=PIECE):
                act.wait_ge(raw_loaded[pos % RAW], 32 * (LP // RAW * layer + 2 * it + pos // RAW + 1))
                act.wait_ge(slot_free, LP * layer + SLOTS * it + pos + 1)
                nc.scalar.activation(w_hi[:, pos % SLOTS, 0:n], raw[:, pos % RAW, 0:n], ACT.Copy).then_inc(hi_done, 1)

            def ahead(layer, pos):
                for p_ in range(AHEAD):
                    split_hi(layer, pos + p_)

            def squares(q, tt):
                act.wait_ge(x_new, 4 * q + 2 * tt + 2)
                nc.scalar.activation(junk.bitcast(BF16)[:, tt * D:(tt + 1) * D], x[:, tt, :], ACT.Square, accum_out=ssq[:, tt:tt + 1]).then_inc(sq_done, 1)

            def enter(layer, s):
                q = 3 * layer + s
                for tt in range(TT):
                    for half in range(2):
                        act.wait_ge(xT_psum, 4 * q + 2 * tt + half + 1)
                        nc.scalar.activation(xT_hi[:, 4 * half:4 * half + 4, tt * P:(tt + 1) * P],
                                             tp[half][:, :].rearrange("p (k n) -> p k n", k=4), ACT.Copy).then_inc(xT_hi_done, 1)
                    squares(q, tt)

            def ffn(layer, f, base):
                s0 = STEPS * (2 * layer + f)

                def silu(s_, tt, it, pos):
                    if tt == 0:
                        act.wait_ge(gu_ready, s_ + 1)
                    else:
                        act.wait_ge(slot_free, SLOTS + LP * layer + SLOTS * it + base + pos + 1)
                    nc.scalar.activation(silu_g[:, tt, :], gu[tt][:, 0:CH], ACT.Silu, scale=rstd[:, tt:tt + 1]).then_inc(silu_done, 1)

                def hidden_hi(e, par, tt):
                    act.wait_ge(hT_psum, e + 1)
                    nc.scalar.activation(aT_hi[:, 2 * par:2 * par + 2, tt * P:(tt + 1) * P],
                                         tp[tt][:, 0:CH].rearrange("p (k n) -> p k n", k=2), ACT.Copy).then_inc(hT_hi_done, 1)

                def step(s_, par, it, pos, nxt):
                    e = 2 * s_
                    silu(s_, 0, it, pos)
                    for p_ in nxt[0:1]:
                        split_hi(layer, base + p_, it)
                    silu(s_, 1, it, pos)
                    hidden_hi(e, par, 0)
                    for p_ in nxt[1:2]:
                        split_hi(layer, base + p_, it)
                    if nxt[2:]:
                        hidden_hi(e + 1, par, 1)
                        for p_ in nxt[2:]:
                            split_hi(layer, base + p_, it)

                act.wait_ge(rstd_done, TT * (3 * layer + 2 * f) + TT)
                step(s0, 0, 0, 1, [2, 3, 4])
                step(s0 + 1, 1, 0, 3, [5, 6, 7])
                with act.Fori(0, LOOPED) as it:
                    for u in range(2):
                        step(s0 + 2 * it + 2 + u, u, it, 6 + 3 * u, [8 + 3 * u, 9 + 3 * u, 10 + 3 * u])
                step(s0 + STEPS - 1, 0, 0, FFN_PIECES - 3, [FFN_PIECES - 1])
                if f == 0:
                    ahead(layer, MIX0)
                else:
                    with act.If(layer < DEPTH - 1):
                        ahead(layer, LP)
                hidden_hi(2 * (s0 + STEPS - 1) + 1, 0, 1)

            def head_squares(n, src, done):
                dst, half = h_ssq[:, 4 * n:4 * n + 4], n % 2
                for i in range(4):
                    ins = nc.scalar.activation(junk[:, (4 * half + i) * P:(4 * half + i + 1) * P], src[:, i * P:(i + 1) * P], ACT.Square, accum_out=dst[:, i:i + 1])
                ins.then_inc(done, 1)

            def mixer(layer):
                def read_proj(c, tt, dst, func=ACT.Copy):
                    if tt == 0:
                        act.wait_ge(proj_ready, PROJ * layer + c + 1)
                    else:
                        act.wait_ge(slot_free, SLOTS + LP * layer + MIX0 + (2 * c + 2 if c < PROJ - 1 else W0))
                    nc.scalar.activation(dst, gu[tt][:, :], func, scale=rstd[:, tt:tt + 1]).then_inc(proj_read, 1)

                def exps(h):
                    act.wait_ge(negmax_done, HEADS * layer + h + 1)
                    for t, (a, b) in enumerate(((0, 256), (256, 384))):
                        for c in range(2):
                            i = (h % 2) * 4 + 2 * t + c
                            ins = nc.scalar.activation(z(h, c, a, b), z(h, c, a, b), ACT.Exp, bias=nmx[:, i:i + 1],
                                                       accum_out=sums[:, i:i + 1])
                    ins.then_inc(exp_done, 1)

                def read_probsT(h):
                    act.wait_ge(probsT_psum, HEADS * layer + h + 1)
                    nc.scalar.activation(probsT(h, 0, 384), tp[h % 2][:, 0:384], ACT.Copy).then_inc(probsT_done, 1)

                def mixed_hi(n, dst, src):
                    act.wait_ge(mT_psum, 4 * layer + n + 1)
                    nc.scalar.activation(dst, src[:, :].rearrange("p (k n) -> p k n", k=4), ACT.Copy).then_inc(mT_hi_done, 1)

                def prep(pos, n=PIECE):
                    split_hi(layer, MIX0 + pos, 0, n)

                act.wait_ge(rstd_done, TT * (3 * layer + 1) + TT)
                prep(2)
                for c, dst in enumerate((dq_dk[:, :, 0:512], dq_dk[:, :, 512:1024], dv[:, :, :])):
                    for tt in range(TT):
                        prep(2 * c + 3 + tt)
                        read_proj(c, tt, dst[:, tt, :])
                for tt in range(TT):
                    prep(9 + tt, PIECE if tt == 0 else PIECE // 2)
                    exps(tt)
                    read_proj(3, tt, rqk[:, tt, :])
                read_probsT(0)
                read_probsT(1)
                for tt in range(TT):
                    prep(11 + tt, PIECE // 2)
                    read_proj(4, tt, rv[:, tt, :])
                    exps(2 + tt)
                act.wait_ge(pv_ready, 2 * layer + 1)
                head_squares(0, gu[1], o_sq_done)
                read_probsT(2)
                read_probsT(3)
                prep(13, PIECE // 2)
                prep(14)
                read_proj(5, 0, gate[:, 0, :], ACT.Silu)
                act.wait_ge(pv_ready, 2 * layer + 2)
                head_squares(1, acc[0], o_sq_done)
                for tt in range(TT):
                    act.wait_ge(o_rstd_done, 2 * layer + tt + 1)
                    act.wait_ge(ro_ready, 2 * layer + tt + 1)
                    head_squares(2 + tt, tp[tt], ro_sq_done)
                prep(15)
                for tt in range(TT):
                    mixed_hi(tt, aT_hi[:, :, tt * P:(tt + 1) * P], acc[2 + tt])
                read_proj(5, 1, gate[:, 1, :], ACT.Silu)
                prep(16)
                prep(17)
                mixed_hi(2, xT_hi[:, 4:8, 0:P], tp[0])
                ahead(layer, FFN2)
                mixed_hi(3, xT_hi[:, 4:8, P:SEQ], tp[1])

            ahead(0, 0)
            act.wait_ge(pool_steps, 3)
            for h in range(HEADS):
                nc.scalar.activation(decay[:, h, :], decay[:, h, :], ACT.Exp, scale=LOG_DECAY[h]).then_inc(decay_exp, 1)
            act.wait_ge(lam_steps, 1 + 2 * DEPTH)
            nc.scalar.activation(lam_exp, lam_dot, ACT.Exp).then_inc(lam_exped, 1)
            with act.Fori(0, DEPTH) as layer:
                enter(layer, 0)
                ffn(layer, 0, 0)
                enter(layer, 1)
                mixer(layer)
                enter(layer, 2)
                ffn(layer, 1, FFN2)
            for tt in range(TT):
                squares(3 * DEPTH, tt)

        @block.vector
        def _(dve):
            def split_lo(layer, pos, it=0, n=PIECE):
                dve.wait_ge(hi_done, LP * layer + SLOTS * it + pos + 1)
                nc.vector.tensor_tensor(w_lo[:, pos % SLOTS, 0:n], raw[:, pos % RAW, 0:n],
                                        w_hi[:, pos % SLOTS, 0:n].bitcast(F32), ALU.subtract).then_inc(lo_done, 1)

            def ahead(layer, pos):
                for p_ in range(AHEAD):
                    split_lo(layer, pos + p_)

            def lo_of(dst, src, hi, done):
                nc.vector.tensor_tensor(dst, src, hi.bitcast(F32), ALU.subtract).then_inc(done, 1)

            def residual(q, tt, factor, used):
                if tt == 0:
                    dve.wait_ge(acc_ready, q + 1)
                else:
                    dve.wait_ge(slot_free, SLOTS + used)
                dve.wait_ge(gain_loaded, 16 * (q + 1))
                for half in range(2):
                    cols = slice(half * 512, (half + 1) * 512)
                    nc.vector.scalar_tensor_tensor(x[:, tt, cols], acc[2 * tt + half][:, :], factor, x[:, tt, cols],
                                                   ALU.mult, ALU.add).then_inc(x_new, 1)
                    dve.wait_ge(x_new, 4 * q + 2 * tt + half + 1)
                    nc.vector.tensor_tensor(wide[:, tt, cols], x[:, tt, cols], gain[:, cols], ALU.mult).then_inc(xg_ready, 1)

            def enter(layer, s, factor):
                q = 3 * layer + s
                for tt in range(TT):
                    residual(q, tt, factor, LP * layer + (0, MIX0, FFN2)[s])
                    for half in range(2):
                        dve.wait_ge(xT_hi_done, 4 * q + 2 * tt + half + 1)
                        ks = slice(4 * half, 4 * half + 4)
                        lo_of(xT_lo[:, ks, tt * P:(tt + 1) * P], tp[half][:, :].rearrange("p (k n) -> p k n", k=4),
                              xT_hi[:, ks, tt * P:(tt + 1) * P], xT_lo_done)

            def ffn(layer, f, base):
                e0 = 2 * STEPS * (2 * layer + f)

                def hide(e, tt):
                    dve.wait_ge(silu_done, e + 1)
                    nc.vector.scalar_tensor_tensor(hidden[:, tt, :], gu[tt][:, CH:2 * CH], rstd[:, tt:tt + 1], silu_g[:, tt, :],
                                                   ALU.mult, ALU.mult).then_inc(hidden_done, 1)

                def hidden_lo(e, par, tt):
                    dve.wait_ge(hT_hi_done, e + 1)
                    ks = slice(2 * par, 2 * par + 2)
                    lo_of(aT_lo[:, ks, tt * P:(tt + 1) * P], tp[tt][:, 0:CH].rearrange("p (k n) -> p k n", k=2),
                          aT_hi[:, ks, tt * P:(tt + 1) * P], hT_lo_done)

                def step(e, par, it, nxt):
                    hide(e, 0)
                    for p_ in nxt[0:1]:
                        split_lo(layer, base + p_, it)
                    hide(e + 1, 1)
                    hidden_lo(e, par, 0)
                    for p_ in nxt[1:2]:
                        split_lo(layer, base + p_, it)
                    if nxt[2:]:
                        hidden_lo(e + 1, par, 1)
                        for p_ in nxt[2:]:
                            split_lo(layer, base + p_, it)

                step(e0, 0, 0, [2, 3, 4])
                step(e0 + 2, 1, 0, [5, 6, 7])
                with dve.Fori(0, LOOPED) as it:
                    for u in range(2):
                        step(e0 + 4 * it + 4 + 2 * u, u, it, [8 + 3 * u, 9 + 3 * u, 10 + 3 * u])
                step(e0 + 2 * (STEPS - 1), 0, 0, [FFN_PIECES - 1])
                if f == 0:
                    ahead(layer, MIX0)
                else:
                    with dve.If(layer < DEPTH - 1):
                        ahead(layer, LP)
                hidden_lo(e0 + 2 * STEPS - 1, 0, 1)

            def mixer(layer):
                def prep(pos, n=PIECE):
                    split_lo(layer, MIX0 + pos, 0, n)

                def read_qkT(n, dst):
                    dve.wait_ge(qkT_psum, 6 * layer + n + 1)
                    nc.vector.tensor_copy(dst, tp[n % 2][:, :].rearrange("p (k n) -> p k n", k=4)).then_inc(qkT_done, 1)

                def biased_max(h):
                    dve.wait_ge(scores_ready, HEADS * layer + h + 1)
                    dve.sem_inc(scores_seen, 1)
                    dve.wait_ge(consts_made, 3)
                    for t, (a, b) in enumerate(((0, 256), (256, 384))):
                        for c in range(2):
                            i = (h % 2) * 4 + 2 * t + c
                            nc.vector.tensor_tensor_reduce(
                                out=z(h, c, a, b), in0=acc[2 * (h % 2) + c][:, a:b], in1=bias8[:, h, SEQ - (b - a):SEQ],
                                scale=SCALE, scalar=MASKED, op0=ALU.add, op1=ALU.max,
                                accum_out=mx[:, i:i + 1]).then_inc(max_done, 1)
                    hs = slice((h % 2) * 4, (h % 2) * 4 + 4)
                    dve.wait_ge(max_done, 4 * (HEADS * layer + h + 1))
                    nc.vector.tensor_scalar(nmx[:, hs], mx[:, hs], -1.0, None, ALU.mult).then_inc(negmax_done, 1)

                def probs(h):
                    hs = slice((h % 2) * 4, (h % 2) * 4 + 4)
                    g = HEADS * layer + h
                    dve.wait_ge(exp_done, g + 1)
                    nc.vector.reciprocal(rec[:, hs], sums[:, hs]).then_inc(rec_steps, 1)
                    dve.wait_ge(rec_steps, 2 * g + 1)
                    odd = rec[:, (h % 2) * 4 + 1:(h % 2) * 4 + 4:2]
                    nc.vector.tensor_scalar(odd, odd, neg_lam, None, ALU.mult).then_inc(rec_steps, 1)
                    for t, (a, b) in enumerate(((0, 256), (256, 384))):
                        i = (h % 2) * 4 + 2 * t
                        nc.vector.tensor_scalar(z(h, 0, a, b), z(h, 0, a, b), rec[:, i:i + 1], None, ALU.mult).then_inc(probs_part, 1)
                    dve.wait_ge(rec_steps, 2 * g + 2)
                    for t, (a, b) in enumerate(((0, 256), (256, 384))):
                        i = (h % 2) * 4 + 2 * t + 1
                        dve.wait_ge(probs_part, 2 * g + t + 1)
                        nc.vector.scalar_tensor_tensor(z(h, 0, a, b), z(h, 1, a, b), rec[:, i:i + 1], z(h, 0, a, b),
                                                       ALU.mult, ALU.add).then_inc(probs_done, 1)

                def diff_norm(pair, src):
                    dve.wait_ge(o_rstd_done, 2 * layer + pair + 1)
                    for t in range(TT):
                        for hh in range(2):
                            i = 2 * t + hh
                            ins = nc.vector.scalar_tensor_tensor(
                                dv[:, t, (2 * pair + hh) * V:(2 * pair + hh + 1) * V], src[:, i * V:(i + 1) * V],
                                h_rstd[:, 4 * pair + i:4 * pair + i + 1], gsub[:, :], ALU.mult, ALU.mult)
                    ins.then_inc(o_done, 1)

                def mixed_lo(n, dst, hi, src):
                    dve.wait_ge(mT_hi_done, 4 * layer + n + 1)
                    lo_of(dst, src[:, :].rearrange("p (k n) -> p k n", k=4), hi, mT_lo_done)

                for n in (2, 3, 4):
                    prep(n)
                for n, t in enumerate((qT, qT, kT, kT)):
                    prep(5 + n)
                    read_qkT(n, t[:, :, (n % 2) * P:(n % 2 + 1) * P])
                biased_max(0)
                biased_max(1)
                for tt in range(TT):
                    prep(9 + tt, PIECE if tt == 0 else PIECE // 2)
                    probs(tt)
                for h in (2, 3):
                    dve.wait_ge(probsT_psum, HEADS * layer + h - 1)
                    biased_max(h)
                prep(11, PIECE // 2)
                for tt in range(TT):
                    read_qkT(4 + tt, rT[:, :, tt * P:(tt + 1) * P])
                probs(2)
                prep(12, PIECE // 2)
                probs(3)
                for h in range(HEADS):
                    dve.wait_ge(ret_ready, HEADS * layer + h + 1)
                    nc.vector.tensor_tensor(retT(h, 0, SEQ), acc[h][:, 0:SEQ], decay[:, h, :], ALU.mult)
                    nc.vector.tensor_tensor(retT(h, SEQ, 384), acc[h][:, SEQ:384], decay[:, h, 0:P], ALU.mult).then_inc(retT_done, 1)
                diff_norm(0, gu[1])
                prep(13, PIECE // 2)
                prep(14)
                diff_norm(1, acc[0])
                prep(15)
                for tt in range(TT):
                    mixed_lo(tt, aT_lo[:, :, tt * P:(tt + 1) * P], aT_hi[:, :, tt * P:(tt + 1) * P], acc[2 + tt])
                for tt in range(TT):
                    dve.wait_ge(ro_rstd_done, 2 * layer + tt + 1)
                    dve.wait_ge(proj_read, 2 * PROJ * layer + 2 * PROJ - 1 + tt)
                    for h in range(HEADS):
                        vs = slice(h * V, (h + 1) * V)
                        ins = nc.vector.scalar_tensor_tensor(rv[:, tt, vs], tp[tt][:, vs], h_rstd[:, 8 + 4 * tt + h:9 + 4 * tt + h],
                                                             gate[:, tt, vs], ALU.mult, ALU.mult)
                    ins.then_inc(ro_done, 1)
                prep(16)
                prep(17)
                mixed_lo(2, xT_lo[:, 4:8, 0:P], xT_hi[:, 4:8, 0:P], tp[0])
                ahead(layer, FFN2)
                mixed_lo(3, xT_lo[:, 4:8, P:SEQ], xT_hi[:, 4:8, P:SEQ], tp[1])

            nc.vector.memset(junk[:, 0:256], 0.0).then_inc(lam_steps, 1)
            ahead(0, 0)
            dve.wait_ge(lam_loaded, 16 * 5)
            for l in range(DEPTH):
                for m in range(2):
                    cols = slice(l * QK, (l + 1) * QK)
                    nc.vector.tensor_tensor_reduce(out=hid[:, (2 * l + m) * QK:(2 * l + m + 1) * QK], in0=lams[:, 2 * m, cols],
                                                   in1=lams[:, 2 * m + 1, cols], scale=1.0, scalar=0.0, op0=ALU.mult, op1=ALU.add,
                                                   accum_out=lam_dot[:, 2 * m + l:2 * m + l + 1]).then_inc(lam_steps, 1)
            for l in range(DEPTH):
                nc.vector.tensor_scalar(gsub2[:, l, :], gsub2[:, l, :], 1.0 - LAM_INIT[l], None, ALU.mult).then_inc(lam_steps, 1)
            dve.wait_ge(lam_exped, 1)
            nc.vector.tensor_tensor(neg_lams, lam_exp[:, DEPTH:2 * DEPTH], lam_exp[:, 0:DEPTH], ALU.subtract).then_inc(lam_steps, 1)
            dve.wait_ge(lam_steps, 2 + 3 * DEPTH)
            for l in range(DEPTH):
                nc.vector.tensor_scalar(neg_lams[:, l:l + 1], neg_lams[:, l:l + 1], -LAM_INIT[l], None, ALU.add).then_inc(lam_steps, 1)
            dve.wait_ge(x_loaded, 16)
            with dve.Fori(0, DEPTH) as layer:
                enter(layer, 0, 0.5)
                dve.wait_ge(rstd_done, TT * (3 * layer) + TT)
                dve.wait_ge(lam_steps, 2 + 4 * DEPTH)
                nc.vector.tensor_copy(neg_lam, neg_lams[:, bass.ds(layer, 1)]).then_inc(layer_vals, 1)
                nc.vector.tensor_copy(gsub[:, :], gsub2[:, bass.ds(layer, 1), :].rearrange("p l n -> p (l n)")).then_inc(layer_vals, 1)
                ffn(layer, 0, 0)
                enter(layer, 1, 0.5)
                dve.wait_ge(layer_vals, 2 * layer + 2)
                mixer(layer)
                enter(layer, 2, 1.0)
                ffn(layer, 1, FFN2)
            q = 3 * DEPTH
            for tt in range(TT):
                residual(q, tt, 0.5, LP * DEPTH)
            for tt in range(TT):
                dve.wait_ge(rstd_done, TT * q + tt + 1)
                dve.wait_ge(xg_ready, 4 * q + 2 * tt + 2)
                nc.vector.tensor_scalar(x[:, tt, :], wide[:, tt, :], rstd[:, tt:tt + 1], None, ALU.mult).then_inc(xg_ready, 1)

        @block.tensor
        def _(pe):
            def three(out_, s_hi, s_lo, m_hi, m_lo, first, last):
                nc.tensor.matmul(out_, s_hi, m_hi, start=first, stop=False)
                nc.tensor.matmul(out_, s_hi, m_lo, start=False, stop=False)
                return nc.tensor.matmul(out_, s_lo, m_hi, start=False, stop=last)

            def piece_ready(layer, pos, it=0):
                pe.wait_ge(lo_done, LP * layer + SLOTS * it + pos + 1 + RAW)

            def enter_T(q, tt):
                for half in range(2):
                    pe.wait_ge(xg_ready, 4 * q + 2 * tt + half + 1)
                    if tt:
                        pe.wait_ge(xT_lo_done, 4 * q + half + 1)
                    for k in range(4):
                        c = (4 * half + k) * P
                        ins = nc.tensor.transpose(tp[half][:, k * P:(k + 1) * P], wide[:, tt, c:c + P], ident[:, :])
                    ins.then_inc(xT_psum, 1)

            def project(layer, it, tt, pos, n_pieces, ready, hook=None, entry=None):
                kk = KT // n_pieces
                for h in range(n_pieces):
                    slot = (pos + h) % SLOTS
                    if tt == 0:
                        piece_ready(layer, pos + h, it)
                    for k in range(kk):
                        kt = h * kk + k
                        if entry is not None and kt in (0, KT // 2):
                            pe.wait_ge(xT_lo_done, 4 * entry + 2 * tt + (kt > 0) + 1)
                        if hook and kt == KT // 2:
                            hook()
                        cs, ts = slice(k * 512, (k + 1) * 512), slice(tt * P, (tt + 1) * P)
                        ins = three(gu[tt][:, :], xT_hi[:, kt, ts], xT_lo[:, kt, ts], w_hi[:, slot, cs], w_lo[:, slot, cs],
                                    kt == 0, kt == KT - 1)
                    if tt == 1:
                        ins.then_inc(slot_free, 1)
                if tt == 0:
                    ins.then_inc(ready, 1)

            def add_rows(layer, it, tt, pos, src_hi, src_lo, k0, first=False, last=False):
                if tt == 0:
                    piece_ready(layer, pos, it)
                slot = pos % SLOTS
                for k in range(2):
                    for half in range(2):
                        cs, ts = slice(k * D + half * 512, k * D + (half + 1) * 512), slice(tt * P, (tt + 1) * P)
                        ins = three(acc[2 * tt + half][:, :], src_hi[:, k0 + k, ts], src_lo[:, k0 + k, ts],
                                    w_hi[:, slot, cs], w_lo[:, slot, cs], first and k == 0, last and k == 1)
                if tt == 1:
                    ins.then_inc(slot_free, 1)
                elif last:
                    ins.then_inc(acc_ready, 1)

            def ffn(layer, f, base):
                e0 = 2 * STEPS * (2 * layer + f)
                q = 3 * layer + 2 * f

                def up(e, it, pos, tt, hook=None, guard=True, entry=None):
                    if guard:
                        pe.wait_ge(hidden_done, e - 1)
                    project(layer, it, tt, base + pos, 2, gu_ready, hook, entry)

                def hidden_T(e, tt, guard=True):
                    pe.wait_ge(hidden_done, e + 1)
                    if guard:
                        pe.wait_ge(hT_lo_done, e - 1)
                    for k in range(2):
                        ins = nc.tensor.transpose(tp[tt][:, k * P:(k + 1) * P], hidden[:, tt, k * P:(k + 1) * P], ident[:, :])
                    ins.then_inc(hT_psum, 1)

                def down(e, it, pos, par, tt, **kw):
                    pe.wait_ge(hT_lo_done, e + 1)
                    add_rows(layer, it, tt, base + pos, aT_hi, aT_lo, 2 * par, **kw)

                up(e0, 0, 0, 0, lambda: enter_T(q, 1), guard=False, entry=q)
                up(e0 + 1, 0, 0, 1, guard=False, entry=q)
                hidden_T(e0, 0, guard=False)
                up(e0 + 2, 0, 2, 0, lambda: hidden_T(e0 + 1, 1, guard=False))
                up(e0 + 3, 0, 2, 1)
                for tt in range(TT):
                    hidden_T(e0 + 2 + tt, tt)
                    down(e0 + tt, 0, 4, 0, tt, first=True)
                with pe.Fori(0, LOOPED) as it:
                    for u in range(2):
                        e = e0 + 4 * it + 4 + 2 * u
                        for tt in range(TT):
                            up(e + tt, it, 5 + 3 * u, tt)
                        for tt in range(TT):
                            hidden_T(e + tt, tt)
                            down(e - 2 + tt, it, 7 + 3 * u, 1 - u, tt)
                e, p_ = e0 + 2 * (STEPS - 1), FFN_PIECES - 4
                for tt in range(TT):
                    up(e + tt, 0, p_, tt)
                for tt in range(TT):
                    hidden_T(e + tt, tt)
                    down(e - 2 + tt, 0, p_ + 2, 1, tt)
                    if tt:
                        enter_T(q + 1, 0)
                    down(e + tt, 0, p_ + 3, 0, tt, last=True)

            def mixer(layer):
                q = 3 * layer + 1
                n_read = 2 * PROJ * layer

                def block_of(c, tt, hook=None):
                    if c:
                        pe.wait_ge(proj_read, n_read + 2 * c - 1 + tt)
                    project(layer, 0, tt, MIX0 + 2 * c, 2 if c < PROJ - 1 else 4, proj_ready, hook, None if c else q)

                def transposes(dst, srcs, done):
                    for i, src in enumerate(srcs):
                        ins = nc.tensor.transpose(dst[:, i * P:(i + 1) * P], src, ident[:, :])
                    ins.then_inc(done, 1)

                def four(src):
                    return [src[:, i * P:(i + 1) * P] for i in range(4)]

                def scores(h):
                    for a, b, qt in ((0, SEQ, 1), (SEQ, 384, 0)):
                        for c in range(2):
                            rows = slice(c * QK, (c + 1) * QK)
                            ins = nc.tensor.matmul(acc[2 * (h % 2) + c][:, a:b], qT[rows, h, qt * P:(qt + 1) * P],
                                                   kT[rows, h, 0:b - a], start=True, stop=True)
                    ins.then_inc(scores_ready, 1)

                def transpose_probs(h):
                    pe.wait_ge(probs_done, 2 * (HEADS * layer + h) + 2)
                    transposes(tp[h % 2], [z(h, 0, i * P, (i + 1) * P) for i in range(3)], probsT_psum)

                def causal(dst, done):
                    for cols, pairs in dst:
                        for i, (blk, vt) in enumerate(pairs):
                            ins = nc.tensor.matmul(cols, blk, vt, start=i == 0, stop=i == len(pairs) - 1)
                    ins.then_inc(done, 1)

                def diff_out(pair, bank):
                    todo = []
                    for t in range(TT):
                        for hh in range(2):
                            h = 2 * pair + hh
                            vs = slice(h * V, (h + 1) * V)
                            pairs = [(probsT(h, 256, 384), dv[:, 0, vs])] if t == 0 else \
                                [(probsT(h, 0, 128), dv[:, 0, vs]), (probsT(h, 128, 256), dv[:, 1, vs])]
                            todo.append((bank[:, (2 * t + hh) * V:(2 * t + hh + 1) * V], pairs))
                    causal(todo, pv_ready)

                def qk_T(c, tt):
                    pe.wait_ge(proj_read, n_read + 2 * c - 1 + tt)
                    if c == 2:
                        pe.wait_ge(qkT_done, 6 * layer + tt + 1)
                    transposes(tp[tt], four(dq_dk[:, tt, (c - 1) * 512:c * 512]), qkT_psum)

                block_of(0, 0, lambda: enter_T(q, 1))
                block_of(0, 1)
                for c in (1, 2):
                    for tt in range(TT):
                        block_of(c, tt, lambda: qk_T(c, tt))
                pe.wait_ge(qkT_done, 6 * layer + 4)
                scores(0)
                scores(1)
                block_of(3, 0)
                block_of(3, 1)
                transpose_probs(0)
                transpose_probs(1)
                for h in (2, 3):
                    pe.wait_ge(negmax_done, HEADS * layer + h - 1)
                    scores(h)
                block_of(4, 0)
                for tt in range(TT):
                    pe.wait_ge(proj_read, n_read + 7 + tt)
                    pe.wait_ge(probsT_done, HEADS * layer + tt + 1)
                    transposes(tp[tt], four(rqk[:, tt, :]), qkT_psum)
                block_of(4, 1)
                pe.wait_ge(qkT_done, 6 * layer + 6)
                pe.wait_ge(negmax_done, HEADS * layer + 4)
                for h in range(HEADS):
                    rows = slice((h % 2) * QK, (h % 2 + 1) * QK)
                    nc.tensor.matmul(acc[h][:, 0:SEQ], rT[rows, 2 + h // 2, 0:P], rT[rows, h // 2, :], start=True, stop=True)
                    nc.tensor.matmul(acc[h][:, SEQ:384], rT[rows, 2 + h // 2, P:SEQ], rT[rows, h // 2, P:SEQ],
                                     start=True, stop=True).then_inc(ret_ready, 1)
                pe.wait_ge(proj_read, n_read + 10)
                diff_out(0, gu[1])
                transpose_probs(2)
                transpose_probs(3)
                block_of(5, 0)
                pe.wait_ge(probsT_done, HEADS * layer + 4)
                pe.wait_ge(retT_done, HEADS * layer + 4)
                diff_out(1, acc[0])
                for t in range(TT):
                    todo = []
                    for h in range(HEADS):
                        vs = slice(h * V, (h + 1) * V)
                        pairs = [(retT(h, 0, 128), rv[:, 0, vs])] if t == 0 else \
                            [(retT(h, 128, 256), rv[:, 0, vs]), (retT(h, 256, 384), rv[:, 1, vs])]
                        todo.append((tp[t][:, vs], pairs))
                    causal(todo, ro_ready)
                pe.wait_ge(o_done, 2 * layer + 1)

                def diff_T():
                    pe.wait_ge(o_done, 2 * layer + 2)
                    for tt in range(TT):
                        transposes(acc[2 + tt], four(dv[:, tt, :]), mT_psum)

                block_of(5, 1, diff_T)
                for tt in range(TT):
                    pe.wait_ge(mT_lo_done, 4 * layer + tt + 1)
                    for w in range(2):
                        add_rows(layer, 0, tt, MIX0 + W0 + w, aT_hi, aT_lo, 2 * w, first=w == 0)
                    pe.wait_ge(ro_done, 2 * layer + tt + 1)
                    transposes(tp[tt], four(rv[:, tt, :]), mT_psum)
                for tt in range(TT):
                    pe.wait_ge(mT_lo_done, 4 * layer + tt + 3)
                    for w in (2, 3):
                        if tt and w == 3:
                            enter_T(q + 1, 0)
                        add_rows(layer, 0, tt, MIX0 + W0 + w, xT_hi, xT_lo, 2 * w, last=w == 3)

            pe.wait_ge(lam_steps, 1)
            for i, bank in enumerate(acc):
                ins = nc.tensor.matmul(bank[:, :], zeros[:, 0:P], zeros, start=True, stop=True)
                if i == 2:
                    ins.then_inc(slot_free, SLOTS)
            ins.then_inc(acc_ready, 1)
            pe.wait_ge(consts_made, 1)
            enter_T(0, 0)
            with pe.Fori(0, DEPTH) as layer:
                ffn(layer, 0, 0)
                mixer(layer)
                ffn(layer, 1, FFN2)


_INS = ['x', 'norm_ffn1', 'w1_gate', 'w1_up', 'w1_down', 'norm_mix', 'w_in', 'lambda_q1', 'lambda_k1', 'lambda_q2',
        'lambda_k2', 'diff_subln', 'w_out', 'norm_ffn2', 'w2_gate', 'w2_up', 'w2_down', 'norm_final']


def kernel(**inputs):
    import numpy as _np
    import concourse.bacc as _bacc
    from concourse import mybir as _mybir
    from concourse.bass_utils import run_bass_kernel_spmd as _run

    nc = _bacc.Bacc("TRN2", target_bir_lowering=False, num_devices=1)
    arrays, args = {}, []
    for name in _INS:
        a = _np.ascontiguousarray(inputs[name])
        arrays[f"in_{name}_dram"] = a
        args.append(nc.dram_tensor(f"in_{name}_dram", a.shape, _mybir.dt.from_np(a.dtype), kind="ExternalInput").ap())
    out = nc.dram_tensor("out_0_dram", (1, 256, 1024), _mybir.dt.float32, kind="ExternalOutput").ap()
    build(nc, *args, out)
    r = _run(nc, [arrays], core_ids=[0])
    return r.results[0]["out_0_dram"]
```

```python
from contextlib import ExitStack

import numpy as np
import concourse.bass as bass
from concourse import mybir

F32 = mybir.dt.float32
F32R = mybir.dt.float32r
BF16 = mybir.dt.bfloat16
ALU = mybir.AluOpType
ACT = mybir.ActivationFunctionType

P = 128
D, SEQ, DEPTH = 1024, 256, 2
TT = SEQ // P
KT = D // P
F = ((8 * D // 3 + 255) // 256) * 256
CH = 256
STEPS = F // CH
HEADS = 4
QK = D // 16
V = 2 * QK
EPS = 1e-6
MASKED = -3.0e38
SCALE = QK ** -0.5

PIECE = 2048
RAW, SLOTS = 3, 6
AHEAD = 2
FFN_PIECES = 3 * STEPS
PROJ = 6
MIX_PIECES = 2 * (PROJ - 1) + 4 + 4
MIX0 = FFN_PIECES
FFN2 = MIX0 + MIX_PIECES
LP = FFN2 + FFN_PIECES
assert LP % SLOTS == 0 and STEPS % 2 == 1
LOOPED = (STEPS - 3) // 2
W0 = 2 * (PROJ - 1) + 4

SLOPES = [2.0 ** (-8.0 * (h + 1) / HEADS) for h in range(HEADS)]
LOG_DECAY = [float(np.log(1.0 - 2.0 ** (-5.0 - h))) for h in range(HEADS)]
LAM_INIT = [0.8 - 0.6 * float(np.exp(-0.3 * l)) for l in range(DEPTH)]


def build(nc, x_in, norm_ffn1, w1_gate, w1_up, w1_down, norm_mix, w_in, lam_q1, lam_k1, lam_q2, lam_k2,
          subln, w_out, norm_ffn2, w2_gate, w2_up, w2_down, norm_final, out):
    ctx = ExitStack()
    with ctx:
        def sb(name, shape, dt=F32):
            return ctx.enter_context(nc.sbuf_tensor(name, shape, dt))

        def sem(name):
            return ctx.enter_context(nc.semaphore(name))

        raw = sb("raw", [P, RAW, PIECE])
        w_hi = sb("w_hi", [P, SLOTS, PIECE], F32R)
        w_lo = sb("w_lo", [P, SLOTS, PIECE], F32R)
        x = sb("x", [P, TT, D])
        wide = sb("wide", [P, TT, D])
        xT_hi = sb("xT_hi", [P, KT, SEQ], F32R)
        xT_lo = sb("xT_lo", [P, KT, SEQ], F32R)
        aT_hi = sb("aT_hi", [P, 4, SEQ], F32R)
        aT_lo = sb("aT_lo", [P, 4, SEQ], F32R)
        gain = sb("gain", [P, D])
        hid = sb("hid", [P, 1024])
        silu_g = hid[:, 0:512].rearrange("p (t n) -> p t n", t=TT)
        hidden = hid[:, 512:1024].rearrange("p (t n) -> p t n", t=TT)
        dv = sb("dv", [P, TT, 512])
        rqk = sb("rqk", [P, TT, 512])
        rv = sb("rv", [P, TT, 512])
        gate = sb("gate", [P, TT, 512])
        qT = sb("qT", [P, HEADS, SEQ])
        kT = sb("kT", [P, HEADS, SEQ])
        rT = sb("rT", [P, 4, SEQ])
        bias8 = sb("bias8", [P, HEADS, SEQ])
        decay = sb("decay", [P, HEADS, SEQ])
        ident = sb("ident", [P, P])
        lams = qT[:, 0:2, :].rearrange("p a (b n) -> p (a b) n", b=2)
        gsub2 = sb("gsub2", [P, DEPTH, V])
        gsub = sb("gsub", [P, V])
        st = sb("st", [P, 64])
        ssq, rstd, tmp = st[:, 0:2], st[:, 2:4], st[:, 4:8]
        neg_half = st[:, 8:12]
        lam_dot, lam_exp, neg_init, neg_lam = st[:, 12:16], st[:, 16:20], st[:, 20:22], st[:, 22:23]
        mx, nmx, sums, rec = (st[:, a:a + 8] for a in (24, 32, 40, 48))
        hn = sb("hn", [P, 48])
        h_ssq, h_tmp, h_rstd = hn[:, 0:16], hn[:, 16:32], hn[:, 32:48]
        junk = rT[:, :, :].rearrange("p a n -> p (a n)")
        dq_dk = wide

        def z(h, c, a, b):
            o = ((h % 2) * 2 + c) * 384
            return wide[:, :, :].rearrange("p t n -> p (t n)")[:, o + a:o + b]

        def probsT(h, a, b):
            t = (qT, kT)[h % 2]
            return t[:, 2 * (h // 2):2 * (h // 2) + 2, :].rearrange("p a n -> p (a n)")[:, a:b]

        def retT(h, a, b):
            t = hid[:, :] if h < 2 else rqk[:, :, :].rearrange("p t n -> p (t n)")
            return t[:, (h % 2) * 384 + a:(h % 2) * 384 + b]

        acc = [ctx.enter_context(nc.psum_tensor(f"acc{i}", [P, 512], F32)) for i in range(4)]
        gu = [ctx.enter_context(nc.psum_tensor(f"gu{i}", [P, 512], F32)) for i in range(2)]
        tp = [ctx.enter_context(nc.psum_tensor(f"tp{i}", [P, 512], F32)) for i in range(2)]

        raw_loaded = [sem(f"raw_loaded{i}") for i in range(RAW)]
        x_loaded = [sem(f"x_loaded{i}") for i in range(TT)]
        gain0_loaded = sem("gain0_loaded")
        lam_loaded, gain_loaded, out_stored = (sem(n) for n in ("lam_loaded", "gain_loaded", "out_stored"))
        consts_made, pool_steps, decay_exp, lam_steps, lam_exped = (
            sem(n) for n in ("consts_made", "pool_steps", "decay_exp", "lam_steps", "lam_exped"))
        hi_done = sem("hi_done")
        lo_done = sem("lo_done")
        slot_free = sem("slot_free")
        acc_ready, x_new, xg_ready, sq_done, rstd_done, xT_psum, xT_hi_done, xT_lo_done = (
            sem(n) for n in ("acc_ready", "x_new", "xg_ready", "sq_done", "rstd_done", "xT_psum", "xT_hi_done", "xT_lo_done"))
        rstd_tmp, normed = sem("rstd_tmp"), sem("normed")
        gu_ready, silu_done, hidden_done, hT_psum, hT_hi_done, hT_lo_done = (
            sem(n) for n in ("gu_ready", "silu_done", "hidden_done", "hT_psum", "hT_hi_done", "hT_lo_done"))
        proj_ready, proj_read = sem("proj_ready"), sem("proj_read")
        qkT_psum, qkT_done = sem("qkT_psum"), sem("qkT_done")
        scores_ready, max_done, negmax_done, exp_done, rec_steps, probs_part, probs_done = (
            sem(n) for n in ("scores_ready", "max_done", "negmax_done", "exp_done", "rec_steps", "probs_part", "probs_done"))
        probsT_psum, probsT_done, pv_ready, o_sq_done, o_rstd_done, o_done = (
            sem(n) for n in ("probsT_psum", "probsT_done", "pv_ready", "o_sq_done", "o_rstd_done", "o_done"))
        ret_ready, retT_done, ro_ready, ro_sq_done, ro_rstd_done, ro_done = (
            sem(n) for n in ("ret_ready", "retT_done", "ro_ready", "ro_sq_done", "ro_rstd_done", "ro_done"))
        head_tmp = sem("head_tmp")
        mT_psum, mT_hi_done, mT_lo_done = sem("mT_psum"), sem("mT_hi_done"), sem("mT_lo_done")
        layer_vals, scores_seen = sem("layer_vals"), sem("scores_seen")

        block = ctx.enter_context(nc.Block())

        @block.sync
        def _(sp):
            sp.sem_inc(lo_done, RAW)
            sp.dma_start(x[:, 0, :], x_in[0, 0:P, :]).then_inc(x_loaded[0], 16)

            def load(layer, it, pos, srcs, n=PIECE):
                sp.wait_ge(lo_done, LP * layer + SLOTS * it + pos + 1)
                dst = raw[:, pos % RAW, 0:n]
                for half, src in enumerate(srcs):
                    if len(srcs[0].shape) == 3 and srcs[0].shape[1] == 4:
                        d = dst.rearrange("p (k g n) -> p k g n", k=4, g=2)[:, :, half, :]
                    else:
                        d = dst[:, half * n // 2:(half + 1) * n // 2]
                        if len(src.shape) == 3:
                            d = d.rearrange("p (k n) -> p k n", k=src.shape[1])
                    sp.dma_start(d, src).then_inc(raw_loaded[pos % RAW], 16)

            def ffn(layer, base, wg, wu, wd):
                def load_gu(it, pos, j):
                    for h in range(2):
                        rows = [w[layer, h * 512:(h + 1) * 512, bass.ds(j * CH, CH)].rearrange("(k p) n -> p k n", p=P)
                                for w in (wg, wu)]
                        load(layer, it, base + pos + h, rows)

                def load_down(it, pos, j):
                    load(layer, it, base + pos, [wd[layer, bass.ds(j * CH + k * P, P), :] for k in range(2)])

                load_gu(0, 0, 0)
                load_gu(0, 2, 1)
                load_down(0, 4, 0)
                with sp.Fori(0, LOOPED) as it:
                    for u in range(2):
                        load_gu(it, 5 + 3 * u, 2 * it + 2 + u)
                        load_down(it, 7 + 3 * u, 2 * it + 1 + u)
                e = FFN_PIECES - 4
                load_gu(0, e, STEPS - 1)
                load_down(0, e + 2, STEPS - 2)
                load_down(0, e + 3, STEPS - 1)

            with sp.Fori(0, DEPTH) as layer:
                ffn(layer, 0, w1_gate, w1_up, w1_down)
                for c in range(PROJ):
                    parts = 2 if c < PROJ - 1 else 4
                    kk = KT // parts
                    for h in range(parts):
                        srcs = [w_in[layer, (h * kk + g * kk // 2) * P:(h * kk + (g + 1) * kk // 2) * P,
                                     c * 512:(c + 1) * 512] for g in range(2)]
                        if kk == 4:
                            srcs = [s.rearrange("(k p) n -> p k n", p=P) for s in srcs]
                        load(layer, 0, MIX0 + 2 * c + h, srcs, kk * 512)
                for w in range(4):
                    load(layer, 0, MIX0 + W0 + w, [w_out[layer, (2 * w + k) * P:(2 * w + k + 1) * P, :] for k in range(2)])
                ffn(layer, FFN2, w2_gate, w2_up, w2_down)
            for i in range(2 * TT):
                tt, cols = i // 2, slice(i % 2 * 512, (i % 2 + 1) * 512)
                sp.wait_ge(normed, i + 1)
                sp.dma_start(out[0, tt * P:(tt + 1) * P, cols], x[:, tt, cols]).then_inc(out_stored, 16)
            sp.wait_ge(out_stored, 16 * 2 * TT)

        @block.gpsimd
        def _(pool):
            def load_gain(src):
                pool.dma_start(gain[:, :], src.partition_broadcast(P)).then_inc(gain_loaded, 16)

            def entry(q, tt):
                pool.wait_ge(sq_done, TT * q + tt + 1)
                nc.gpsimd.tensor_scalar(tmp[:, tt:tt + 1], ssq[:, tt:tt + 1], 1.0 / D, EPS, ALU.mult, ALU.add).then_inc(rstd_tmp, 1)
                pool.wait_ge(rstd_tmp, TT * q + tt + 1)
                nc.gpsimd.tensor_tensor(rstd[:, tt:tt + 1], tmp[:, tt:tt + 1], neg_half[:, 0:1], ALU.pow).then_inc(rstd_done, 1)

            def head_factor(layer, i, when, count, done):
                fs = slice(4 * i, 4 * i + 4)
                pool.wait_ge(when, count)
                nc.gpsimd.tensor_scalar(h_tmp[:, fs], h_ssq[:, fs], 1.0 / V, EPS, ALU.mult, ALU.add).then_inc(head_tmp, 1)
                pool.wait_ge(head_tmp, 4 * layer + i + 1)
                nc.gpsimd.tensor_tensor(h_rstd[:, fs], h_tmp[:, fs], neg_half, ALU.pow).then_inc(done, 1)

            nc.gpsimd.memset(ident[:, :], 0.0).then_inc(pool_steps, 1)
            nc.gpsimd.memset(neg_half, -0.5).then_inc(pool_steps, 1)
            pool.wait_ge(pool_steps, 2)
            nc.gpsimd.affine_select(out=ident[:, :], in_=ident[:, :], compare_op=ALU.not_equal, fill=1.0, base=0,
                                    pattern=[[-1, P]], channel_multiplier=1).then_inc(consts_made, 1)
            nc.gpsimd.iota(decay[:, :, :], pattern=[[0, HEADS], [1, SEQ]], base=0, channel_multiplier=-1,
                           allow_small_or_imprecise_dtypes=True).then_inc(pool_steps, 1)
            for i, lam in enumerate((lam_q1, lam_k1, lam_q2, lam_k2)):
                pool.dma_start(lams[:, i, :], lam.rearrange("l n -> (l n)").partition_broadcast(P)).then_inc(lam_loaded, 16)
            pool.dma_start(gsub2[:, :, :].rearrange("p l n -> p (l n)"),
                           subln.rearrange("l n -> (l n)").partition_broadcast(P)).then_inc(lam_loaded, 16)
            for l in range(DEPTH):
                nc.gpsimd.memset(neg_init[:, l:l + 1], -LAM_INIT[l]).then_inc(pool_steps, 1)
            for tt in range(TT):
                entry(0, tt)
            nc.gpsimd.iota(bias8[:, :, :], pattern=[[0, HEADS], [-1, SEQ]], base=P, channel_multiplier=1,
                           allow_small_or_imprecise_dtypes=True).then_inc(pool_steps, 1)
            pool.wait_ge(pool_steps, 4 + DEPTH)
            for h in range(HEADS):
                nc.gpsimd.tensor_scalar(bias8[:, h, :], bias8[:, h, :], -SLOPES[h] / SCALE, None, ALU.mult).then_inc(pool_steps, 1)
            pool.wait_ge(decay_exp, HEADS)
            nc.gpsimd.tensor_scalar(decay[:, :, :], decay[:, :, :], SCALE, None, ALU.mult).then_inc(pool_steps, 1)
            pool.wait_ge(pool_steps, 5 + HEADS + DEPTH)
            nc.gpsimd.affine_select(out=bias8[:, :, :], in_=bias8[:, :, :], compare_op=ALU.is_ge, fill=MASKED, base=P,
                                    pattern=[[0, HEADS], [-1, SEQ]], channel_multiplier=1).then_inc(consts_made, 1)
            nc.gpsimd.affine_select(out=decay[:, :, :], in_=decay[:, :, :], compare_op=ALU.is_ge, fill=0.0, base=0,
                                    pattern=[[0, HEADS], [1, SEQ]], channel_multiplier=-1).then_inc(consts_made, 1)

            def next_gain(q, src):
                pool.wait_ge(xg_ready, 4 * q + 4)
                load_gain(src)

            def mixer_and_ffn2_entry(layer):
                for tt in range(TT):
                    entry(3 * layer + 1, tt)
                next_gain(3 * layer + 1, norm_ffn2[layer, :])
                for pair in range(2):
                    head_factor(layer, pair, o_sq_done, 2 * layer + pair + 1, o_rstd_done)
                for tt in range(TT):
                    head_factor(layer, 2 + tt, ro_sq_done, 2 * layer + tt + 1, ro_rstd_done)
                for tt in range(TT):
                    entry(3 * layer + 2, tt)

            next_gain(0, norm_mix[0, :])
            mixer_and_ffn2_entry(0)
            if DEPTH > 1:
                with pool.Fori(1, DEPTH) as layer:
                    next_gain(3 * layer - 1, norm_ffn1[layer, :])
                    for tt in range(TT):
                        entry(3 * layer, tt)
                    next_gain(3 * layer, norm_mix[layer, :])
                    mixer_and_ffn2_entry(layer)
            next_gain(3 * DEPTH - 1, norm_final[:])
            for tt in range(TT):
                entry(3 * DEPTH, tt)

        @block.scalar
        def _(act):
            def split_hi(layer, pos, it=0, n=PIECE):
                act.wait_ge(raw_loaded[pos % RAW], 32 * (LP // RAW * layer + 2 * it + pos // RAW + 1))
                act.wait_ge(slot_free, LP * layer + SLOTS * it + pos + 1)
                nc.scalar.activation(w_hi[:, pos % SLOTS, 0:n], raw[:, pos % RAW, 0:n], ACT.Copy).then_inc(hi_done, 1)

            def ahead(layer, pos, some=range(AHEAD)):
                for p_ in some:
                    split_hi(layer, pos + p_)

            def ahead_after(layer, f, some):
                if f == 0:
                    ahead(layer, MIX0, some)
                else:
                    with act.If(layer < DEPTH - 1):
                        ahead(layer, LP, some)

            def squares(q, tt):
                if isinstance(q, int) and q == 0:
                    act.wait_ge(x_loaded[tt], 16)
                else:
                    act.wait_ge(x_new, 4 * (q - 1) + 2 * tt + 2)
                nc.scalar.activation(junk.bitcast(BF16)[:, tt * D:(tt + 1) * D], x[:, tt, :], ACT.Square,
                                     accum_out=ssq[:, tt:tt + 1]).then_inc(sq_done, 1)

            def xT_parts(q, tt):
                for half in range(2):
                    act.wait_ge(xT_psum, 4 * q + 2 * tt + half + 1)
                    nc.scalar.activation(xT_hi[:, 4 * half:4 * half + 4, tt * P:(tt + 1) * P],
                                         tp[half][:, :].rearrange("p (k n) -> p k n", k=4), ACT.Copy).then_inc(xT_hi_done, 1)

            def enter(q):
                for tt in range(TT):
                    xT_parts(q, tt)
                    squares(q, tt)

            def ffn(layer, f, base):
                s0 = STEPS * (2 * layer + f)

                def silu(s_, tt, it, pos):
                    if tt == 0:
                        act.wait_ge(gu_ready, s_ + 1)
                    else:
                        act.wait_ge(slot_free, SLOTS + LP * layer + SLOTS * it + base + pos + 1)
                    nc.scalar.activation(silu_g[:, tt, :], gu[tt][:, 0:CH], ACT.Silu, scale=rstd[:, tt:tt + 1]).then_inc(silu_done, 1)

                def hidden_hi(e, par, tt):
                    act.wait_ge(hT_psum, e + 1)
                    nc.scalar.activation(aT_hi[:, 2 * par:2 * par + 2, tt * P:(tt + 1) * P],
                                         tp[tt][:, 0:CH].rearrange("p (k n) -> p k n", k=2), ACT.Copy).then_inc(hT_hi_done, 1)

                def step(s_, par, it, pos, nxt):
                    silu(s_, 0, it, pos)
                    nxt(0)
                    silu(s_, 1, it, pos)
                    hidden_hi(2 * s_, par, 0)
                    nxt(1)
                    hidden_hi(2 * s_ + 1, par, 1)
                    nxt(2)

                def pieces(it, *lots):
                    return lambda i: None if lots[i] is None else split_hi(layer, base + lots[i], it)

                def last_lots(i):
                    if i == 0:
                        split_hi(layer, base + FFN_PIECES - 1)
                        ahead_after(layer, f, [0])
                    elif i == 1:
                        ahead_after(layer, f, [1])

                split_hi(layer, base + 2)
                act.wait_ge(rstd_done, TT * (3 * layer + 2 * f) + TT)
                step(s0, 0, 0, 1, pieces(0, 3, 4, None))
                step(s0 + 1, 1, 0, 3, pieces(0, 5, 6, 7))
                with act.Fori(0, LOOPED) as it:
                    for u in range(2):
                        p_ = 8 + 3 * u
                        step(s0 + 2 * it + 2 + u, u, it, 6 + 3 * u, pieces(it, p_, p_ + 1, p_ + 2))
                step(s0 + STEPS - 1, 0, 0, FFN_PIECES - 3, last_lots)

            def head_squares(n, src, done):
                dst, half = h_ssq[:, 4 * n:4 * n + 4], n % 2
                for i in range(4):
                    ins = nc.scalar.activation(junk[:, (4 * half + i) * P:(4 * half + i + 1) * P], src[:, i * P:(i + 1) * P], ACT.Square,
                                               accum_out=dst[:, i:i + 1])
                ins.then_inc(done, 1)

            def mixer(layer):
                def read_proj(c, tt, dst, func=ACT.Copy):
                    if tt == 0:
                        act.wait_ge(proj_ready, PROJ * layer + c + 1)
                    else:
                        act.wait_ge(slot_free, SLOTS + LP * layer + MIX0 + (2 * c + 2 if c < PROJ - 1 else W0))
                    nc.scalar.activation(dst, gu[tt][:, :], func, scale=rstd[:, tt:tt + 1]).then_inc(proj_read, 1)

                def exps(h):
                    act.wait_ge(negmax_done, HEADS * layer + h + 1)
                    for t, (a, b) in enumerate(((0, 256), (256, 384))):
                        for c in range(2):
                            i = (h % 2) * 4 + 2 * t + c
                            ins = nc.scalar.activation(z(h, c, a, b), z(h, c, a, b), ACT.Exp, bias=nmx[:, i:i + 1],
                                                       accum_out=sums[:, i:i + 1])
                    ins.then_inc(exp_done, 1)

                def read_probsT(h):
                    act.wait_ge(probsT_psum, HEADS * layer + h + 1)
                    nc.scalar.activation(probsT(h, 0, 384), tp[h % 2][:, 0:384], ACT.Copy).then_inc(probsT_done, 1)

                def mixed_hi(n, dst, src):
                    act.wait_ge(mT_psum, 4 * layer + n + 1)
                    nc.scalar.activation(dst, src[:, :].rearrange("p (k n) -> p k n", k=4), ACT.Copy).then_inc(mT_hi_done, 1)

                def prep(pos, n=PIECE):
                    split_hi(layer, MIX0 + pos, 0, n)

                act.wait_ge(rstd_done, TT * (3 * layer + 1) + TT)
                prep(2)
                for c, dst in enumerate((dq_dk[:, :, 0:512], dq_dk[:, :, 512:1024], dv[:, :, :])):
                    for tt in range(TT):
                        prep(2 * c + 3 + tt)
                        read_proj(c, tt, dst[:, tt, :])
                act.wait_ge(lam_steps, 2 * DEPTH)
                own = bass.ds(2 * layer, 2)
                nc.scalar.activation(lam_exp[:, own], lam_dot[:, own], ACT.Exp).then_inc(lam_exped, 1)
                for tt in range(TT):
                    prep(9 + tt, PIECE if tt == 0 else PIECE // 2)
                    exps(tt)
                    read_proj(3, tt, rqk[:, tt, :])
                read_probsT(0)
                read_probsT(1)
                for tt in range(TT):
                    prep(11 + tt, PIECE // 2)
                    read_proj(4, tt, rv[:, tt, :])
                    exps(2 + tt)
                prep(13, PIECE // 2)
                act.wait_ge(pv_ready, 2 * layer + 1)
                head_squares(0, gu[1], o_sq_done)
                read_probsT(2)
                read_probsT(3)
                prep(14)
                read_proj(5, 0, gate[:, 0, :], ACT.Silu)
                act.wait_ge(pv_ready, 2 * layer + 2)
                head_squares(1, acc[0], o_sq_done)
                for tt in range(TT):
                    act.wait_ge(o_rstd_done, 2 * layer + tt + 1)
                    act.wait_ge(ro_ready, 2 * layer + tt + 1)
                    head_squares(2 + tt, tp[tt], ro_sq_done)
                prep(15)
                for tt in range(TT):
                    mixed_hi(tt, aT_hi[:, :, tt * P:(tt + 1) * P], acc[2 + tt])
                read_proj(5, 1, gate[:, 1, :], ACT.Silu)
                prep(16)
                prep(17)
                mixed_hi(2, xT_hi[:, 4:8, 0:P], tp[0])
                ahead(layer, FFN2)
                mixed_hi(3, xT_hi[:, 4:8, P:SEQ], tp[1])

            act.dma_start(gain[:, :], norm_ffn1[0, :].partition_broadcast(P)).then_inc(gain0_loaded, 16)
            act.wait_ge(pool_steps, 3)
            for h in range(HEADS):
                nc.scalar.activation(decay[:, h, :], decay[:, h, :], ACT.Exp, scale=LOG_DECAY[h]).then_inc(decay_exp, 1)
            xT_parts(0, 0)
            act.wait_ge(raw_loaded[0], 32)
            act.dma_start(x[:, 1, :], x_in[0, P:2 * P, :]).then_inc(x_loaded[1], 16)
            ahead(0, 0)
            for tt in range(TT):
                squares(0, tt)
            xT_parts(0, 1)
            with act.Fori(0, DEPTH) as layer:
                ffn(layer, 0, 0)
                enter(3 * layer + 1)
                mixer(layer)
                enter(3 * layer + 2)
                ffn(layer, 1, FFN2)
                with act.If(layer < DEPTH - 1):
                    enter(3 * layer + 3)
            for tt in range(TT):
                squares(3 * DEPTH, tt)

        @block.vector
        def _(dve):
            def split_lo(layer, pos, it=0, n=PIECE):
                dve.wait_ge(hi_done, LP * layer + SLOTS * it + pos + 1)
                nc.vector.tensor_tensor(w_lo[:, pos % SLOTS, 0:n], raw[:, pos % RAW, 0:n],
                                        w_hi[:, pos % SLOTS, 0:n].bitcast(F32), ALU.subtract).then_inc(lo_done, 1)

            def ahead(layer, pos, some=range(AHEAD)):
                for p_ in some:
                    split_lo(layer, pos + p_)

            def ahead_after(layer, f, some):
                if f == 0:
                    ahead(layer, MIX0, some)
                else:
                    with dve.If(layer < DEPTH - 1):
                        ahead(layer, LP, some)

            def lo_of(dst, src, hi, done):
                nc.vector.tensor_tensor(dst, src, hi.bitcast(F32), ALU.subtract).then_inc(done, 1)

            def residual(q, tt, factor, used):
                if factor is None:
                    dve.wait_ge(x_loaded[tt], 16)
                    dve.wait_ge(gain0_loaded, 16)
                else:
                    dve.wait_ge(gain_loaded, 16 * q)
                for half in range(2):
                    cols = slice(half * 512, (half + 1) * 512)
                    if factor is not None:
                        if (tt, half) != (1, 1):
                            dve.wait_ge(acc_ready, 3 * (q - 1) + 2 * tt + half + 1)
                        else:
                            dve.wait_ge(slot_free, SLOTS + used)
                        nc.vector.scalar_tensor_tensor(x[:, tt, cols], acc[2 * tt + half][:, :], factor, x[:, tt, cols],
                                                       ALU.mult, ALU.add).then_inc(x_new, 1)
                        dve.wait_ge(x_new, 4 * (q - 1) + 2 * tt + half + 1)
                    nc.vector.tensor_tensor(wide[:, tt, cols], x[:, tt, cols], gain[:, cols], ALU.mult).then_inc(xg_ready, 1)

            def xT_parts(q, tt):
                for half in range(2):
                    dve.wait_ge(xT_hi_done, 4 * q + 2 * tt + half + 1)
                    ks = slice(4 * half, 4 * half + 4)
                    lo_of(xT_lo[:, ks, tt * P:(tt + 1) * P], tp[half][:, :].rearrange("p (k n) -> p k n", k=4),
                          xT_hi[:, ks, tt * P:(tt + 1) * P], xT_lo_done)

            def enter(q, factor, used):
                for tt in range(TT):
                    residual(q, tt, factor, used)
                    xT_parts(q, tt)

            def ffn(layer, f, base):
                e0 = 2 * STEPS * (2 * layer + f)

                def hide(e, tt):
                    dve.wait_ge(silu_done, e + 1)
                    nc.vector.scalar_tensor_tensor(hidden[:, tt, :], gu[tt][:, CH:2 * CH], rstd[:, tt:tt + 1], silu_g[:, tt, :],
                                                   ALU.mult, ALU.mult).then_inc(hidden_done, 1)

                def hidden_lo(e, par, tt):
                    dve.wait_ge(hT_hi_done, e + 1)
                    ks = slice(2 * par, 2 * par + 2)
                    lo_of(aT_lo[:, ks, tt * P:(tt + 1) * P], tp[tt][:, 0:CH].rearrange("p (k n) -> p k n", k=2),
                          aT_hi[:, ks, tt * P:(tt + 1) * P], hT_lo_done)

                def step(e, par, it, nxt):
                    hide(e, 0)
                    nxt(0)
                    hide(e + 1, 1)
                    hidden_lo(e, par, 0)
                    nxt(1)
                    hidden_lo(e + 1, par, 1)
                    nxt(2)

                def pieces(it, *lots):
                    return lambda i: None if lots[i] is None else split_lo(layer, base + lots[i], it)

                def last_lots(i):
                    if i == 0:
                        split_lo(layer, base + FFN_PIECES - 1)
                        ahead_after(layer, f, [0])
                    elif i == 1:
                        ahead_after(layer, f, [1])

                split_lo(layer, base + 2)
                step(e0, 0, 0, pieces(0, 3, 4, None))
                step(e0 + 2, 1, 0, pieces(0, 5, 6, 7))
                with dve.Fori(0, LOOPED) as it:
                    for u in range(2):
                        p_ = 8 + 3 * u
                        step(e0 + 4 * it + 4 + 2 * u, u, it, pieces(it, p_, p_ + 1, p_ + 2))
                step(e0 + 2 * (STEPS - 1), 0, 0, last_lots)

            def mixer(layer):
                def prep(pos, n=PIECE):
                    split_lo(layer, MIX0 + pos, 0, n)

                def read_qkT(n, dst):
                    dve.wait_ge(qkT_psum, 6 * layer + n + 1)
                    nc.vector.tensor_copy(dst, tp[n % 2][:, :].rearrange("p (k n) -> p k n", k=4)).then_inc(qkT_done, 1)

                def biased_max(h):
                    dve.wait_ge(scores_ready, HEADS * layer + h + 1)
                    dve.sem_inc(scores_seen, 1)
                    dve.wait_ge(consts_made, 3)
                    for t, (a, b) in enumerate(((0, 256), (256, 384))):
                        for c in range(2):
                            i = (h % 2) * 4 + 2 * t + c
                            nc.vector.tensor_tensor_reduce(
                                out=z(h, c, a, b), in0=acc[2 * (h % 2) + c][:, a:b], in1=bias8[:, h, SEQ - (b - a):SEQ],
                                scale=SCALE, scalar=MASKED, op0=ALU.add, op1=ALU.max,
                                accum_out=mx[:, i:i + 1]).then_inc(max_done, 1)
                    hs = slice((h % 2) * 4, (h % 2) * 4 + 4)
                    dve.wait_ge(max_done, 4 * (HEADS * layer + h + 1))
                    nc.vector.tensor_scalar(nmx[:, hs], mx[:, hs], -1.0, None, ALU.mult).then_inc(negmax_done, 1)

                def probs(h):
                    hs = slice((h % 2) * 4, (h % 2) * 4 + 4)
                    g = HEADS * layer + h
                    dve.wait_ge(exp_done, g + 1)
                    nc.vector.reciprocal(rec[:, hs], sums[:, hs]).then_inc(rec_steps, 1)
                    dve.wait_ge(rec_steps, 2 * g + 1)
                    odd = rec[:, (h % 2) * 4 + 1:(h % 2) * 4 + 4:2]
                    nc.vector.tensor_scalar(odd, odd, neg_lam, None, ALU.mult).then_inc(rec_steps, 1)
                    for t, (a, b) in enumerate(((0, 256), (256, 384))):
                        i = (h % 2) * 4 + 2 * t
                        nc.vector.tensor_scalar(z(h, 0, a, b), z(h, 0, a, b), rec[:, i:i + 1], None, ALU.mult).then_inc(probs_part, 1)
                    dve.wait_ge(rec_steps, 2 * g + 2)
                    for t, (a, b) in enumerate(((0, 256), (256, 384))):
                        i = (h % 2) * 4 + 2 * t + 1
                        dve.wait_ge(probs_part, 2 * g + t + 1)
                        nc.vector.scalar_tensor_tensor(z(h, 0, a, b), z(h, 1, a, b), rec[:, i:i + 1], z(h, 0, a, b),
                                                       ALU.mult, ALU.add).then_inc(probs_done, 1)

                def diff_norm(pair, src):
                    dve.wait_ge(o_rstd_done, 2 * layer + pair + 1)
                    for t in range(TT):
                        for hh in range(2):
                            i = 2 * t + hh
                            ins = nc.vector.scalar_tensor_tensor(
                                dv[:, t, (2 * pair + hh) * V:(2 * pair + hh + 1) * V], src[:, i * V:(i + 1) * V],
                                h_rstd[:, 4 * pair + i:4 * pair + i + 1], gsub[:, :], ALU.mult, ALU.mult)
                    ins.then_inc(o_done, 1)

                def mixed_lo(n, dst, hi, src):
                    dve.wait_ge(mT_hi_done, 4 * layer + n + 1)
                    lo_of(dst, src[:, :].rearrange("p (k n) -> p k n", k=4), hi, mT_lo_done)

                for n in (2, 3, 4):
                    prep(n)
                for n, t in enumerate((qT, qT, kT, kT)):
                    prep(5 + n)
                    read_qkT(n, t[:, :, (n % 2) * P:(n % 2 + 1) * P])
                biased_max(0)
                biased_max(1)
                dve.wait_ge(lam_exped, layer + 1)
                nc.vector.tensor_tensor(neg_lam, lam_exp[:, bass.ds(2 * layer + 1, 1)], lam_exp[:, bass.ds(2 * layer, 1)],
                                        ALU.subtract).then_inc(layer_vals, 1)
                dve.wait_ge(layer_vals, 3 * layer + 2)
                nc.vector.tensor_tensor(neg_lam, neg_lam, neg_init[:, bass.ds(layer, 1)], ALU.add).then_inc(layer_vals, 1)
                dve.wait_ge(layer_vals, 3 * layer + 3)
                for tt in range(TT):
                    prep(9 + tt, PIECE if tt == 0 else PIECE // 2)
                    probs(tt)
                for h in (2, 3):
                    dve.wait_ge(probsT_psum, HEADS * layer + h - 1)
                    biased_max(h)
                prep(11, PIECE // 2)
                for tt in range(TT):
                    read_qkT(4 + tt, rT[:, :, tt * P:(tt + 1) * P])
                probs(2)
                prep(12, PIECE // 2)
                probs(3)
                for h in range(HEADS):
                    dve.wait_ge(ret_ready, HEADS * layer + h + 1)
                    nc.vector.tensor_tensor(retT(h, 0, SEQ), acc[h][:, 0:SEQ], decay[:, h, :], ALU.mult)
                    nc.vector.tensor_tensor(retT(h, SEQ, 384), acc[h][:, SEQ:384], decay[:, h, 0:P], ALU.mult).then_inc(retT_done, 1)
                prep(13, PIECE // 2)
                diff_norm(0, gu[1])
                prep(14)
                diff_norm(1, acc[0])
                for tt in range(TT):
                    mixed_lo(tt, aT_lo[:, :, tt * P:(tt + 1) * P], aT_hi[:, :, tt * P:(tt + 1) * P], acc[2 + tt])
                    if tt == 0:
                        prep(15)
                for tt in range(TT):
                    dve.wait_ge(ro_rstd_done, 2 * layer + tt + 1)
                    dve.wait_ge(proj_read, 2 * PROJ * layer + 2 * PROJ - 1 + tt)
                    for h in range(HEADS):
                        vs = slice(h * V, (h + 1) * V)
                        ins = nc.vector.scalar_tensor_tensor(rv[:, tt, vs], tp[tt][:, vs], h_rstd[:, 8 + 4 * tt + h:9 + 4 * tt + h],
                                                             gate[:, tt, vs], ALU.mult, ALU.mult)
                    ins.then_inc(ro_done, 1)
                prep(16)
                prep(17)
                mixed_lo(2, xT_lo[:, 4:8, 0:P], xT_hi[:, 4:8, 0:P], tp[0])
                ahead(layer, FFN2)
                mixed_lo(3, xT_lo[:, 4:8, P:SEQ], xT_hi[:, 4:8, P:SEQ], tp[1])

            residual(0, 0, None, 0)
            xT_parts(0, 0)
            ahead(0, 0)
            residual(0, 1, None, 0)
            xT_parts(0, 1)
            dve.wait_ge(lam_loaded, 16 * 5)
            for l in range(DEPTH):
                for m in range(2):
                    cols = slice(l * QK, (l + 1) * QK)
                    nc.vector.tensor_tensor_reduce(out=gate[:, 0, (2 * l + m) * QK:(2 * l + m + 1) * QK], in0=lams[:, 2 * m, cols],
                                                   in1=lams[:, 2 * m + 1, cols], scale=1.0, scalar=0.0, op0=ALU.mult, op1=ALU.add,
                                                   accum_out=lam_dot[:, 2 * l + m:2 * l + m + 1]).then_inc(lam_steps, 1)
            for l in range(DEPTH):
                nc.vector.tensor_scalar(gsub2[:, l, :], gsub2[:, l, :], 1.0 - LAM_INIT[l], None, ALU.mult).then_inc(lam_steps, 1)
            with dve.Fori(0, DEPTH) as layer:
                ffn(layer, 0, 0)
                dve.wait_ge(lam_steps, 3 * DEPTH)
                nc.vector.tensor_copy(gsub[:, :], gsub2[:, bass.ds(layer, 1), :].rearrange("p l n -> p (l n)")).then_inc(layer_vals, 1)
                enter(3 * layer + 1, 0.5, LP * layer + MIX0)
                mixer(layer)
                enter(3 * layer + 2, 1.0, LP * layer + FFN2)
                ffn(layer, 1, FFN2)
                with dve.If(layer < DEPTH - 1):
                    enter(3 * layer + 3, 0.5, LP * layer + LP)
            q = 3 * DEPTH
            for tt in range(TT):
                residual(q, tt, 0.5, LP * DEPTH)
            for tt in range(TT):
                dve.wait_ge(rstd_done, TT * q + tt + 1)
                dve.wait_ge(xg_ready, 4 * q + 2 * tt + 2)
                for half in range(2):
                    cols = slice(half * 512, (half + 1) * 512)
                    nc.vector.tensor_scalar(x[:, tt, cols], wide[:, tt, cols], rstd[:, tt:tt + 1], None, ALU.mult).then_inc(normed, 1)

        @block.tensor
        def _(pe):
            def three(out_, s_hi, s_lo, m_hi, m_lo, first, last):
                nc.tensor.matmul(out_, s_hi, m_hi, start=first, stop=False)
                nc.tensor.matmul(out_, s_hi, m_lo, start=False, stop=False)
                return nc.tensor.matmul(out_, s_lo, m_hi, start=False, stop=last)

            def piece_ready(layer, pos, it=0):
                pe.wait_ge(lo_done, LP * layer + SLOTS * it + pos + 1 + RAW)

            def enter_T(q, tt):
                for half in range(2):
                    pe.wait_ge(xg_ready, 4 * q + 2 * tt + half + 1)
                    if tt:
                        pe.wait_ge(xT_lo_done, 4 * q + half + 1)
                    for k in range(4):
                        c = (4 * half + k) * P
                        ins = nc.tensor.transpose(tp[half][:, k * P:(k + 1) * P], wide[:, tt, c:c + P], ident[:, :])
                    ins.then_inc(xT_psum, 1)

            def project(layer, it, tt, pos, n_pieces, ready, hook=None, entry=None):
                kk = KT // n_pieces
                for h in range(n_pieces):
                    slot = (pos + h) % SLOTS
                    if tt == 0:
                        piece_ready(layer, pos + h, it)
                    for k in range(kk):
                        kt = h * kk + k
                        if entry is not None and kt in (0, KT // 2):
                            pe.wait_ge(xT_lo_done, 4 * entry + 2 * tt + (kt > 0) + 1)
                        if hook and kt == KT // 2:
                            hook()
                        cs, ts = slice(k * 512, (k + 1) * 512), slice(tt * P, (tt + 1) * P)
                        ins = three(gu[tt][:, :], xT_hi[:, kt, ts], xT_lo[:, kt, ts], w_hi[:, slot, cs], w_lo[:, slot, cs],
                                    kt == 0, kt == KT - 1)
                    if tt == 1:
                        ins.then_inc(slot_free, 1)
                if tt == 0:
                    ins.then_inc(ready, 1)

            def add_rows(layer, it, tt, pos, src_hi, src_lo, k0, first=False, last=False):
                if tt == 0:
                    piece_ready(layer, pos, it)
                slot = pos % SLOTS
                for half in range(2):
                    for k in range(2):
                        cs, ts = slice(k * D + half * 512, k * D + (half + 1) * 512), slice(tt * P, (tt + 1) * P)
                        ins = three(acc[2 * tt + half][:, :], src_hi[:, k0 + k, ts], src_lo[:, k0 + k, ts],
                                    w_hi[:, slot, cs], w_lo[:, slot, cs], first and k == 0, last and k == 1)
                    if (tt, half) == (1, 1):
                        ins.then_inc(slot_free, 1)
                    elif last:
                        ins.then_inc(acc_ready, 1)

            def ffn(layer, f, base):
                e0 = 2 * STEPS * (2 * layer + f)
                q = 3 * layer + 2 * f

                def up(e, it, pos, tt, hook=None, guard=True, entry=None):
                    if guard:
                        pe.wait_ge(hidden_done, e - 1)
                    project(layer, it, tt, base + pos, 2, gu_ready, hook, entry)

                def hidden_T(e, tt, guard=True):
                    pe.wait_ge(hidden_done, e + 1)
                    if guard:
                        pe.wait_ge(hT_lo_done, e - 1)
                    for k in range(2):
                        ins = nc.tensor.transpose(tp[tt][:, k * P:(k + 1) * P], hidden[:, tt, k * P:(k + 1) * P], ident[:, :])
                    ins.then_inc(hT_psum, 1)

                def down(e, it, pos, par, tt, **kw):
                    pe.wait_ge(hT_lo_done, e + 1)
                    add_rows(layer, it, tt, base + pos, aT_hi, aT_lo, 2 * par, **kw)

                up(e0, 0, 0, 0, lambda: enter_T(q, 1), guard=False, entry=q)
                up(e0 + 1, 0, 0, 1, guard=False, entry=q)
                hidden_T(e0, 0, guard=False)
                up(e0 + 2, 0, 2, 0, lambda: hidden_T(e0 + 1, 1, guard=False))
                up(e0 + 3, 0, 2, 1)
                for tt in range(TT):
                    hidden_T(e0 + 2 + tt, tt)
                    down(e0 + tt, 0, 4, 0, tt, first=True)
                with pe.Fori(0, LOOPED) as it:
                    for u in range(2):
                        e = e0 + 4 * it + 4 + 2 * u
                        for tt in range(TT):
                            up(e + tt, it, 5 + 3 * u, tt)
                        for tt in range(TT):
                            hidden_T(e + tt, tt)
                            down(e - 2 + tt, it, 7 + 3 * u, 1 - u, tt)
                e, p_ = e0 + 2 * (STEPS - 1), FFN_PIECES - 4
                for tt in range(TT):
                    up(e + tt, 0, p_, tt)
                for tt in range(TT):
                    if tt == 0:
                        hidden_T(e, 0)
                    down(e - 2 + tt, 0, p_ + 2, 1, tt)
                    if tt == 0:
                        hidden_T(e + 1, 1)
                    if tt:
                        enter_T(q + 1, 0)
                    down(e + tt, 0, p_ + 3, 0, tt, last=True)

            def mixer(layer):
                q = 3 * layer + 1
                n_read = 2 * PROJ * layer

                def block_of(c, tt, hook=None):
                    if c:
                        pe.wait_ge(proj_read, n_read + 2 * c - 1 + tt)
                    project(layer, 0, tt, MIX0 + 2 * c, 2 if c < PROJ - 1 else 4, proj_ready, hook, None if c else q)

                def transposes(dst, srcs, done):
                    for i, src in enumerate(srcs):
                        ins = nc.tensor.transpose(dst[:, i * P:(i + 1) * P], src, ident[:, :])
                    ins.then_inc(done, 1)

                def four(src):
                    return [src[:, i * P:(i + 1) * P] for i in range(4)]

                def scores(h):
                    for a, b, qt in ((0, SEQ, 1), (SEQ, 384, 0)):
                        for c in range(2):
                            rows = slice(c * QK, (c + 1) * QK)
                            ins = nc.tensor.matmul(acc[2 * (h % 2) + c][:, a:b], qT[rows, h, qt * P:(qt + 1) * P],
                                                   kT[rows, h, 0:b - a], start=True, stop=True)
                    ins.then_inc(scores_ready, 1)

                def transpose_probs(h):
                    pe.wait_ge(probs_done, 2 * (HEADS * layer + h) + 2)
                    transposes(tp[h % 2], [z(h, 0, i * P, (i + 1) * P) for i in range(3)], probsT_psum)

                def causal(dst, done):
                    for cols, pairs in dst:
                        for i, (blk, vt) in enumerate(pairs):
                            ins = nc.tensor.matmul(cols, blk, vt, start=i == 0, stop=i == len(pairs) - 1)
                    ins.then_inc(done, 1)

                def diff_out(pair, bank):
                    todo = []
                    for t in range(TT):
                        for hh in range(2):
                            h = 2 * pair + hh
                            vs = slice(h * V, (h + 1) * V)
                            pairs = [(probsT(h, 256, 384), dv[:, 0, vs])] if t == 0 else \
                                [(probsT(h, 0, 128), dv[:, 0, vs]), (probsT(h, 128, 256), dv[:, 1, vs])]
                            todo.append((bank[:, (2 * t + hh) * V:(2 * t + hh + 1) * V], pairs))
                    causal(todo, pv_ready)

                def qk_T(c, tt):
                    pe.wait_ge(proj_read, n_read + 2 * c - 1 + tt)
                    if c == 2:
                        pe.wait_ge(qkT_done, 6 * layer + tt + 1)
                    transposes(tp[tt], four(dq_dk[:, tt, (c - 1) * 512:c * 512]), qkT_psum)

                block_of(0, 0, lambda: enter_T(q, 1))
                block_of(0, 1)
                for c in (1, 2):
                    for tt in range(TT):
                        block_of(c, tt, lambda: qk_T(c, tt))
                pe.wait_ge(qkT_done, 6 * layer + 4)
                scores(0)
                scores(1)
                block_of(3, 0)
                block_of(3, 1)
                transpose_probs(0)
                transpose_probs(1)
                for h in (2, 3):
                    pe.wait_ge(negmax_done, HEADS * layer + h - 1)
                    scores(h)
                block_of(4, 0)
                for tt in range(TT):
                    pe.wait_ge(proj_read, n_read + 7 + tt)
                    pe.wait_ge(probsT_done, HEADS * layer + tt + 1)
                    transposes(tp[tt], four(rqk[:, tt, :]), qkT_psum)
                block_of(4, 1)
                pe.wait_ge(qkT_done, 6 * layer + 6)
                pe.wait_ge(negmax_done, HEADS * layer + 4)
                for h in range(HEADS):
                    rows = slice((h % 2) * QK, (h % 2 + 1) * QK)
                    nc.tensor.matmul(acc[h][:, 0:SEQ], rT[rows, 2 + h // 2, 0:P], rT[rows, h // 2, :], start=True, stop=True)
                    nc.tensor.matmul(acc[h][:, SEQ:384], rT[rows, 2 + h // 2, P:SEQ], rT[rows, h // 2, P:SEQ],
                                     start=True, stop=True).then_inc(ret_ready, 1)
                pe.wait_ge(proj_read, n_read + 10)
                diff_out(0, gu[1])
                transpose_probs(2)
                transpose_probs(3)
                block_of(5, 0)
                pe.wait_ge(probsT_done, HEADS * layer + 4)
                pe.wait_ge(retT_done, HEADS * layer + 4)
                diff_out(1, acc[0])
                for t in range(TT):
                    todo = []
                    for h in range(HEADS):
                        vs = slice(h * V, (h + 1) * V)
                        pairs = [(retT(h, 0, 128), rv[:, 0, vs])] if t == 0 else \
                            [(retT(h, 128, 256), rv[:, 0, vs]), (retT(h, 256, 384), rv[:, 1, vs])]
                        todo.append((tp[t][:, vs], pairs))
                    causal(todo, ro_ready)
                pe.wait_ge(o_done, 2 * layer + 1)

                def diff_T():
                    pe.wait_ge(o_done, 2 * layer + 2)
                    for tt in range(TT):
                        transposes(acc[2 + tt], four(dv[:, tt, :]), mT_psum)

                block_of(5, 1, diff_T)
                for tt in range(TT):
                    pe.wait_ge(mT_lo_done, 4 * layer + tt + 1)
                    for w in range(2):
                        add_rows(layer, 0, tt, MIX0 + W0 + w, aT_hi, aT_lo, 2 * w, first=w == 0)
                    pe.wait_ge(ro_done, 2 * layer + tt + 1)
                    transposes(tp[tt], four(rv[:, tt, :]), mT_psum)
                for tt in range(TT):
                    pe.wait_ge(mT_lo_done, 4 * layer + tt + 3)
                    for w in (2, 3):
                        if tt and w == 3:
                            enter_T(q + 1, 0)
                        add_rows(layer, 0, tt, MIX0 + W0 + w, xT_hi, xT_lo, 2 * w, last=w == 3)

            pe.sem_inc(slot_free, SLOTS)
            pe.wait_ge(consts_made, 1)
            enter_T(0, 0)
            with pe.Fori(0, DEPTH) as layer:
                ffn(layer, 0, 0)
                mixer(layer)
                ffn(layer, 1, FFN2)


_INS = ['x', 'norm_ffn1', 'w1_gate', 'w1_up', 'w1_down', 'norm_mix', 'w_in', 'lambda_q1', 'lambda_k1', 'lambda_q2',
        'lambda_k2', 'diff_subln', 'w_out', 'norm_ffn2', 'w2_gate', 'w2_up', 'w2_down', 'norm_final']


def kernel(**inputs):
    import numpy as _np
    import concourse.bacc as _bacc
    from concourse import mybir as _mybir
    from concourse.bass_utils import run_bass_kernel_spmd as _run

    nc = _bacc.Bacc("TRN2", target_bir_lowering=False, num_devices=1)
    arrays, args = {}, []
    for name in _INS:
        a = _np.ascontiguousarray(inputs[name])
        arrays[f"in_{name}_dram"] = a
        args.append(nc.dram_tensor(f"in_{name}_dram", a.shape, _mybir.dt.from_np(a.dtype), kind="ExternalInput").ap())
    out = nc.dram_tensor("out_0_dram", (1, 256, 1024), _mybir.dt.float32, kind="ExternalOutput").ap()
    build(nc, *args, out)
    r = _run(nc, [arrays], core_ids=[0])
    return r.results[0]["out_0_dram"]
```
